# Optimizing a Trainium2 kernel written in Bass

```python
import jax, jax.numpy as jnp
from jax import lax
import numpy as np

D_MODEL = 1024
BATCH = 1
SEQ = 256
DEPTH = 2

ROPE_THETA = 500000.0
EPS = 1e-6
NEG = -1e30
Q_BLOCK = 128

GROUP_WIDTH = D_MODEL // 4
D_MIX = 4 * GROUP_WIDTH

MLA_HEADS = 4
MLA_NOPE = 64
MLA_ROPE = 32
MLA_QK = MLA_NOPE + MLA_ROPE
MLA_V = GROUP_WIDTH // MLA_HEADS
MLA_Q_RANK = 256
MLA_KV_RANK = 128

CONV_WIDTH = 3

SG_CHUNK = 128
SG_GROUPS = 4
SG_GDIM = GROUP_WIDTH // SG_GROUPS

MOBA_HEADS = 4
MOBA_HD = GROUP_WIDTH // MOBA_HEADS
MOBA_ROT = MOBA_HD // 4
MOBA_BLOCK = 256
MOBA_TOPK = 3

SPLIT_SIZES = (
    MLA_Q_RANK, MLA_KV_RANK, MLA_ROPE, GROUP_WIDTH,
    GROUP_WIDTH, GROUP_WIDTH, GROUP_WIDTH, GROUP_WIDTH,
    GROUP_WIDTH, GROUP_WIDTH, GROUP_WIDTH,
    GROUP_WIDTH, GROUP_WIDTH, GROUP_WIDTH, GROUP_WIDTH,
)
D_IN = 3488


def rmsnorm(x, g):
    xf = x.astype(jnp.float32)
    y = xf * lax.rsqrt(jnp.mean(xf * xf, axis=-1, keepdims=True) + EPS)
    return (y * g).astype(x.dtype)

def layernorm(x, g, b):
    xf = x.astype(jnp.float32)
    mu = jnp.mean(xf, axis=-1, keepdims=True)
    var = jnp.mean(jnp.square(xf - mu), axis=-1, keepdims=True)
    y = (xf - mu) * lax.rsqrt(var + EPS)
    return (y * g + b).astype(x.dtype)

def rope(x, pos):
    rd = x.shape[-1]
    half = rd // 2
    inv = jnp.power(ROPE_THETA, -jnp.arange(half, dtype=jnp.float32) * 2.0 / rd)
    ang = pos.astype(jnp.float32)[..., None] * inv
    cos = jnp.cos(ang)[:, :, None, :]
    sin = jnp.sin(ang)[:, :, None, :]
    xf = x.astype(jnp.float32)
    x1, x2 = xf[..., :half], xf[..., half:]
    return jnp.concatenate([x1 * cos - x2 * sin, x2 * cos + x1 * sin], axis=-1).astype(x.dtype)

def causal_attention_blocks(q, k, v, scale):
    B, S, H, D = q.shape
    nq = S // Q_BLOCK
    qb = q.reshape(B, nq, Q_BLOCK, H, D).swapaxes(0, 1)
    kpos = jnp.arange(S)

    def one(args):
        qblk, i = args
        s = jnp.einsum('bqhd,bkhd->bhqk', qblk, k, preferred_element_type=jnp.float32) * scale
        qpos = i * Q_BLOCK + jnp.arange(Q_BLOCK)
        s = jnp.where(kpos[None, :] <= qpos[:, None], s, NEG)
        p = jax.nn.softmax(s, axis=-1)
        return jnp.einsum('bhqk,bkhd->bqhd', p.astype(v.dtype), v)

    out = lax.map(one, (qb, jnp.arange(nq)))
    return out.swapaxes(0, 1).reshape(B, S, H, v.shape[-1])

def moba_attention(q, k, v, scale):
    B, S, H, D = q.shape
    nb = -(-S // MOBA_BLOCK)
    Sp = nb * MOBA_BLOCK
    kk = min(MOBA_TOPK, nb)
    pad = ((0, 0), (0, Sp - S), (0, 0), (0, 0))
    kb = jnp.pad(k, pad).reshape(B, nb, MOBA_BLOCK, H, D).transpose(0, 3, 1, 2, 4)
    vb = jnp.pad(v, pad).reshape(B, nb, MOBA_BLOCK, H, D).transpose(0, 3, 1, 2, 4)
    kmean = jnp.mean(kb.astype(jnp.float32), axis=3)
    gate = jnp.einsum('bshd,bhnd->bhsn', q.astype(jnp.float32), kmean)
    qblk = jnp.arange(S) // MOBA_BLOCK
    past = jnp.arange(nb)[None, :] < qblk[:, None]
    gate = jnp.where(past, gate, NEG)
    _, idx = lax.top_k(gate, kk)
    valid = jnp.arange(kk)[None, :] < qblk[:, None]

    nq = S // Q_BLOCK
    qc = q.reshape(B, nq, Q_BLOCK, H, D).transpose(1, 0, 3, 2, 4)
    idxc = idx.reshape(B, H, nq, Q_BLOCK, kk).transpose(2, 0, 1, 3, 4)
    validc = valid.reshape(nq, Q_BLOCK, kk)
    bi = jnp.arange(B)[:, None, None, None]
    hi = jnp.arange(H)[None, :, None, None]
    n_sel = kk * MOBA_BLOCK

    def one(args):
        qx, ix, vx, i = args
        kg = kb[bi, hi, ix]
        vg = vb[bi, hi, ix]
        s_sel = jnp.einsum('bhqd,bhqrkd->bhqrk', qx, kg, preferred_element_type=jnp.float32) * scale
        s_sel = jnp.where(vx[None, None, :, :, None], s_sel, NEG).reshape(B, H, Q_BLOCK, n_sel)
        qpos = i * Q_BLOCK + jnp.arange(Q_BLOCK)
        own = (i * Q_BLOCK) // MOBA_BLOCK
        ko = lax.dynamic_index_in_dim(kb, own, axis=2, keepdims=False)
        vo = lax.dynamic_index_in_dim(vb, own, axis=2, keepdims=False)
        s_own = jnp.einsum('bhqd,bhkd->bhqk', qx, ko, preferred_element_type=jnp.float32) * scale
        kpos = own * MOBA_BLOCK + jnp.arange(MOBA_BLOCK)
        s_own = jnp.where(kpos[None, :] <= qpos[:, None], s_own, NEG)
        p = jax.nn.softmax(jnp.concatenate([s_sel, s_own], axis=-1), axis=-1).astype(v.dtype)
        p_sel = p[..., :n_sel].reshape(B, H, Q_BLOCK, kk, MOBA_BLOCK)
        p_own = p[..., n_sel:]
        return (jnp.einsum('bhqrk,bhqrkd->bhqd', p_sel, vg)
                + jnp.einsum('bhqk,bhkd->bhqd', p_own, vo))

    out = lax.map(one, (qc, idxc, validc, jnp.arange(nq)))
    return out.transpose(1, 0, 3, 2, 4).reshape(B, S, H, D)

def short_conv(z, w):
    C = z.shape[-1]
    return lax.conv_general_dilated(
        z, w[:, None, :].astype(z.dtype), window_strides=(1,), padding=[(CONV_WIDTH - 1, 0)],
        dimension_numbers=('NWC', 'WIO', 'NWC'), feature_group_count=C)

def spatial_gate(u, v, ln_g, ln_b, w_s, b_s):
    B, S, C = v.shape
    nc = S // SG_CHUNK
    vn = layernorm(v, ln_g, ln_b).reshape(B, nc, SG_CHUNK, SG_GROUPS, SG_GDIM)
    mask = jnp.tril(jnp.ones((SG_CHUNK, SG_CHUNK), dtype=bool))
    ws = jnp.where(mask[None], w_s, jnp.zeros_like(w_s))
    mixed = jnp.einsum('gts,bcsgd->bctgd', ws, vn) + b_s.T[None, None, :, :, None]
    return u * mixed.reshape(B, S, C)

def hybrid_layer(x, positions, norm_g, w_in, mla_q_norm_g, mla_w_uq, mla_kv_norm_g, mla_w_ukv,
                 mla_q_g, mla_k_nope_g, mla_k_rope_g, conv_w, sg_ln_g, sg_ln_b, sg_w, sg_b,
                 moba_q_g, moba_k_g, w_out):
    B, S, _ = x.shape
    h = rmsnorm(x, norm_g)
    p = h @ w_in
    offs = np.cumsum(np.array(SPLIT_SIZES))[:-1].tolist()
    (cq, ckv, kr, g_a, c_h, c_b, c_c, g_b, sg_u, sg_v, g_c, mq, mk, mv, g_d) = jnp.split(p, offs, axis=-1)

    q = (rmsnorm(cq, mla_q_norm_g) @ mla_w_uq).reshape(B, S, MLA_HEADS, MLA_QK)
    kv = (rmsnorm(ckv, mla_kv_norm_g) @ mla_w_ukv).reshape(B, S, MLA_HEADS, MLA_NOPE + MLA_V)
    k_nope, v_a = kv[..., :MLA_NOPE], kv[..., MLA_NOPE:]
    q = rmsnorm(q, mla_q_g)
    q = jnp.concatenate([q[..., :MLA_NOPE], rope(q[..., MLA_NOPE:], positions)], axis=-1)
    k_nope = rmsnorm(k_nope, mla_k_nope_g)
    k_rope = rope(rmsnorm(kr, mla_k_rope_g)[:, :, None, :], positions)
    k = jnp.concatenate([k_nope, jnp.broadcast_to(k_rope, (B, S, MLA_HEADS, MLA_ROPE))], axis=-1)
    o_a = causal_attention_blocks(q, k, v_a, MLA_QK ** -0.5).reshape(B, S, GROUP_WIDTH)

    o_b = c_b * short_conv(c_c * c_h, conv_w)

    o_c = spatial_gate(sg_u, sg_v, sg_ln_g, sg_ln_b, sg_w, sg_b)

    qd = rmsnorm(mq.reshape(B, S, MOBA_HEADS, MOBA_HD), moba_q_g)
    kd = rmsnorm(mk.reshape(B, S, MOBA_HEADS, MOBA_HD), moba_k_g)
    vd = mv.reshape(B, S, MOBA_HEADS, MOBA_HD)
    qd = jnp.concatenate([rope(qd[..., :MOBA_ROT], positions), qd[..., MOBA_ROT:]], axis=-1)
    kd = jnp.concatenate([rope(kd[..., :MOBA_ROT], positions), kd[..., MOBA_ROT:]], axis=-1)
    o_d = moba_attention(qd, kd, vd, MOBA_HD ** -0.5).reshape(B, S, GROUP_WIDTH)

    y = jnp.concatenate([o_a * jax.nn.silu(g_a), o_b * jax.nn.silu(g_b),
                         o_c * jax.nn.silu(g_c), o_d * jax.nn.silu(g_d)], axis=-1)
    return y @ w_out

def first_inputs(seed: int = 0) -> dict:
    key = jax.random.key(seed)
    ks = jax.random.split(key, 24)
    L, D, GW = DEPTH, D_MODEL, GROUP_WIDTH
    f32 = jnp.float32

    def nrm(k, shape, scale):
        return jax.random.normal(k, shape, f32) * scale

    def gain(k, shape):
        return 1.0 + 0.05 * jax.random.normal(k, shape, f32)

    x = jax.random.normal(ks[0], (BATCH, SEQ, D), f32)
    offset = jax.random.randint(ks[1], (BATCH, 1), 0, 4096, dtype=jnp.int32)
    positions = (offset + jnp.arange(SEQ, dtype=jnp.int32)[None, :]).astype(jnp.int32)
    return {
        "x": x,
        "positions": positions,
        "norm_g": gain(ks[2], (L, D)),
        "w_in": nrm(ks[3], (L, D, D_IN), D ** -0.5),
        "mla_q_norm_g": gain(ks[4], (L, MLA_Q_RANK)),
        "mla_w_uq": nrm(ks[5], (L, MLA_Q_RANK, MLA_HEADS * MLA_QK), MLA_Q_RANK ** -0.5),
        "mla_kv_norm_g": gain(ks[6], (L, MLA_KV_RANK)),
        "mla_w_ukv": nrm(ks[7], (L, MLA_KV_RANK, MLA_HEADS * (MLA_NOPE + MLA_V)), MLA_KV_RANK ** -0.5),
        "mla_q_g": gain(ks[8], (L, MLA_QK)),
        "mla_k_nope_g": gain(ks[9], (L, MLA_NOPE)),
        "mla_k_rope_g": gain(ks[10], (L, MLA_ROPE)),
        "conv_w": nrm(ks[11], (L, CONV_WIDTH, GW), CONV_WIDTH ** -0.5),
        "sg_ln_g": gain(ks[12], (L, GW)),
        "sg_ln_b": nrm(ks[13], (L, GW), 0.02),
        "sg_w": nrm(ks[14], (L, SG_GROUPS, SG_CHUNK, SG_CHUNK), SG_CHUNK ** -0.5),
        "sg_b": 1.0 + nrm(ks[15], (L, SG_GROUPS, SG_CHUNK), 0.1),
        "moba_q_g": gain(ks[16], (L, MOBA_HD)),
        "moba_k_g": gain(ks[17], (L, MOBA_HD)),
        "w_out": nrm(ks[18], (L, D_MIX, D), D_MIX ** -0.5),
    }

def first_block(x, positions, norm_g, w_in, mla_q_norm_g, mla_w_uq, mla_kv_norm_g, mla_w_ukv,
              mla_q_g, mla_k_nope_g, mla_k_rope_g, conv_w, sg_ln_g, sg_ln_b, sg_w, sg_b,
              moba_q_g, moba_k_g, w_out):
    for l in range(DEPTH):
        x = x + hybrid_layer(x, positions, norm_g[l], w_in[l], mla_q_norm_g[l], mla_w_uq[l],
                             mla_kv_norm_g[l], mla_w_ukv[l], mla_q_g[l], mla_k_nope_g[l],
                             mla_k_rope_g[l], conv_w[l], sg_ln_g[l], sg_ln_b[l], sg_w[l], sg_b[l],
                             moba_q_g[l], moba_k_g[l], w_out[l])
    return x


D_POOL = D_MODEL // 2
POOL_WINDOWS = (2, 4, 8, 16)
N_POOL_GROUPS = len(POOL_WINDOWS)
POOL_GROUP = D_POOL // N_POOL_GROUPS
D_ATTN = D_MODEL // 2
HEAD_DIM = 64
N_HEADS = D_ATTN // HEAD_DIM
DILATED_PATTERNS = ((128, 1), (512, 4), (2048, 16))
D_IN_2 = D_POOL + 3 * D_ATTN
D_FF = 2816
N_EXPERTS = 8
TOP_K = 2
D_FF_EXPERT = 3584
N_DENSE = (DEPTH + 1) // 2
N_MOE = DEPTH // 2


def rmsnorm_2(x, g):
    xf = x.astype(jnp.float32)
    y = xf * lax.rsqrt(jnp.mean(xf * xf, axis=-1, keepdims=True) + EPS)
    return (y * g.astype(jnp.float32)).astype(x.dtype)

def pool_mixer(u, w_pool, pool_scale):
    B, S, _ = u.shape
    uf = u.astype(jnp.float32)
    c = jnp.concatenate([jnp.zeros((B, 1, D_POOL), jnp.float32), jnp.cumsum(uf, axis=1)], axis=1)
    t = jnp.arange(S)
    diffs = []
    for gi, w in enumerate(POOL_WINDOWS):
        sl = slice(gi * POOL_GROUP, (gi + 1) * POOL_GROUP)
        cg = c[..., sl]
        lo = jnp.maximum(t + 1 - w, 0)
        win_sum = cg[:, 1:] - cg[:, lo]
        cnt = (t + 1 - lo).astype(jnp.float32)[None, :, None]
        diffs.append(win_sum / cnt - uf[..., sl])
    d = jnp.stack(diffs, axis=2).astype(u.dtype)
    z = jnp.einsum('bsgc,gce->bsge', d, w_pool).reshape(B, S, D_POOL)
    return rmsnorm_2(z, pool_scale)

def dilated_attention(q, k, v):
    B, H, S, Dh = q.shape
    nb = S // Q_BLOCK
    scale = HEAD_DIM ** -0.5
    qb = q.reshape(B, H, nb, Q_BLOCK, Dh).transpose(2, 0, 1, 3, 4)

    def block(args):
        bi, qblk = args
        pos = bi * Q_BLOCK + jnp.arange(Q_BLOCK)
        outs, lses = [], []
        for window, dil in DILATED_PATTERNS:
            n_keys = window // dil + 1
            kidx = pos[:, None] - dil * jnp.arange(n_keys)[None, :]
            valid = kidx >= 0
            kidx = jnp.maximum(kidx, 0)
            kg = k[:, :, kidx]
            vg = v[:, :, kidx]
            s = jnp.einsum('bhqd,bhqjd->bhqj', qblk, kg).astype(jnp.float32) * scale
            s = jnp.where(valid[None, None], s, -jnp.inf)
            m = jnp.max(s, axis=-1, keepdims=True)
            p = jnp.exp(s - m)
            den = jnp.sum(p, axis=-1, keepdims=True)
            o = jnp.einsum('bhqj,bhqjd->bhqd', p, vg.astype(jnp.float32)) / den
            outs.append(o)
            lses.append(m + jnp.log(den))
        wts = jax.nn.softmax(jnp.concatenate(lses, axis=-1), axis=-1)
        o = jnp.einsum('bhqp,pbhqd->bhqd', wts, jnp.stack(outs, axis=0))
        return o.astype(q.dtype)

    ob = lax.map(block, (jnp.arange(nb), qb))
    return ob.transpose(1, 2, 0, 3, 4).reshape(B, H, S, Dh)

def hybrid_mixer(h, w_in, w_pool, pool_scale, attn_gain, w_out):
    B, S, _ = h.shape
    proj = h @ w_in
    u = proj[..., :D_POOL]
    q, k, v = jnp.split(proj[..., D_POOL:], 3, axis=-1)
    to_heads = lambda t: t.reshape(B, S, N_HEADS, HEAD_DIM).transpose(0, 2, 1, 3)
    y_a = pool_mixer(u, w_pool, pool_scale)
    o = dilated_attention(to_heads(q), to_heads(k), to_heads(v))
    y_b = rmsnorm_2(o.transpose(0, 2, 1, 3).reshape(B, S, D_ATTN), attn_gain)
    return jnp.concatenate([y_a, y_b], axis=-1) @ w_out

def swiglu(h, wg, wu, wd):
    return (jax.nn.silu(h @ wg) * (h @ wu)) @ wd

def moe_swiglu(h, w_router, wg, wu, wd):
    B, S, D = h.shape
    xt = h.reshape(-1, D)
    logits = (xt @ w_router).astype(jnp.float32)
    top_v, top_i = lax.top_k(logits, TOP_K)
    gates = jax.nn.softmax(top_v, axis=-1)
    gate = jnp.sum(jax.nn.one_hot(top_i, N_EXPERTS, dtype=jnp.float32) * gates[..., None], axis=1)
    y = jnp.zeros_like(xt)
    for e in range(N_EXPERTS):
        y = y + gate[:, e:e + 1].astype(xt.dtype) * swiglu(xt, wg[e], wu[e], wd[e])
    return y.reshape(B, S, D)

def second_inputs(seed: int = 0) -> dict:
    key = jax.random.key(seed)
    ks = jax.random.split(key, 20)
    f32 = jnp.float32
    nrm = lambda k, shape, fan_in: jax.random.normal(k, shape, f32) * (fan_in ** -0.5)
    gain = lambda k, shape: 1.0 + 0.05 * jax.random.normal(k, shape, f32)
    return {
        "x": jax.random.normal(ks[0], (BATCH, SEQ, D_MODEL), f32),
        "norm_mix": gain(ks[1], (DEPTH, D_MODEL)),
        "w_in": nrm(ks[2], (DEPTH, D_MODEL, D_IN_2), D_MODEL),
        "w_pool": nrm(ks[3], (DEPTH, N_POOL_GROUPS, POOL_GROUP, POOL_GROUP), POOL_GROUP),
        "pool_scale": gain(ks[4], (DEPTH, D_POOL)),
        "attn_gain": gain(ks[5], (DEPTH, D_ATTN)),
        "w_out": nrm(ks[6], (DEPTH, D_MODEL, D_MODEL), D_MODEL),
        "norm_ffn": gain(ks[7], (DEPTH, D_MODEL)),
        "ffn_wg": nrm(ks[8], (N_DENSE, D_MODEL, D_FF), D_MODEL),
        "ffn_wu": nrm(ks[9], (N_DENSE, D_MODEL, D_FF), D_MODEL),
        "ffn_wd": nrm(ks[10], (N_DENSE, D_FF, D_MODEL), D_FF),
        "w_router": nrm(ks[11], (N_MOE, D_MODEL, N_EXPERTS), D_MODEL),
        "moe_wg": nrm(ks[12], (N_MOE, N_EXPERTS, D_MODEL, D_FF_EXPERT), D_MODEL),
        "moe_wu": nrm(ks[13], (N_MOE, N_EXPERTS, D_MODEL, D_FF_EXPERT), D_MODEL),
        "moe_wd": nrm(ks[14], (N_MOE, N_EXPERTS, D_FF_EXPERT, D_MODEL), D_FF_EXPERT),
        "final_norm": gain(ks[15], (D_MODEL,)),
    }

def second_block(x, norm_mix, w_in, w_pool, pool_scale, attn_gain, w_out, norm_ffn,
              ffn_wg, ffn_wu, ffn_wd, w_router, moe_wg, moe_wu, moe_wd, final_norm):
    for l in range(DEPTH):
        h = rmsnorm_2(x, norm_mix[l])
        x = x + hybrid_mixer(h, w_in[l], w_pool[l], pool_scale[l], attn_gain[l], w_out[l])
        h = rmsnorm_2(x, norm_ffn[l])
        if l % 2 == 0:
            i = l // 2
            x = x + swiglu(h, ffn_wg[i], ffn_wu[i], ffn_wd[i])
        else:
            i = l // 2
            x = x + moe_swiglu(h, w_router[i], moe_wg[i], moe_wu[i], moe_wd[i])
    return rmsnorm_2(x, final_norm)


def setup_inputs(seed=0):
    out = dict(first_inputs(seed))
    for name, value in second_inputs(seed + 1).items():
        if name != "x":
            out[name + "_2"] = value
    return out


def reference(
    x, positions, norm_g, w_in, mla_q_norm_g, mla_w_uq, mla_kv_norm_g, mla_w_ukv, mla_q_g,
    mla_k_nope_g, mla_k_rope_g, conv_w, sg_ln_g, sg_ln_b, sg_w, sg_b, moba_q_g, moba_k_g, w_out,
    norm_mix_2, w_in_2, w_pool_2, pool_scale_2, attn_gain_2, w_out_2, norm_ffn_2, ffn_wg_2,
    ffn_wu_2, ffn_wd_2, w_router_2, moe_wg_2, moe_wu_2, moe_wd_2, final_norm_2,
):
    x = first_block(
        x, positions, norm_g, w_in, mla_q_norm_g, mla_w_uq, mla_kv_norm_g, mla_w_ukv, mla_q_g,
        mla_k_nope_g, mla_k_rope_g, conv_w, sg_ln_g, sg_ln_b, sg_w, sg_b, moba_q_g, moba_k_g,
        w_out,
    )
    return second_block(
        x, norm_mix_2, w_in_2, w_pool_2, pool_scale_2, attn_gain_2, w_out_2, norm_ffn_2,
        ffn_wg_2, ffn_wu_2, ffn_wd_2, w_router_2, moe_wg_2, moe_wu_2, moe_wd_2, final_norm_2,
    )


_drawn_inputs = setup_inputs


def setup_inputs(seed=0):
    import zlib

    import numpy as np

    out = dict(_drawn_inputs(seed))
    spreads = {}
    factors = {'mla_q_norm_g': 6.355,
     'mla_kv_norm_g': 3.014,
     'mla_q_g': 4.115,
     'mla_k_nope_g': 6.266,
     'mla_k_rope_g': 7.763,
     'sg_ln_b': 4.148,
     'moba_q_g': 5.501,
     'moba_k_g': 7.067}
    for name, (base, spread) in spreads.items():
        noise = np.random.default_rng([zlib.crc32(name.encode()), seed]).standard_normal(out[name].shape)
        drawn = base * np.exp(spread * noise) if base else spread * noise
        out[name] = __import__('jax').numpy.asarray(drawn.astype(out[name].dtype))
    for name, factor in factors.items():
        out[name] = (out[name] * factor).astype(out[name].dtype)
    return out
```

```python
from contextlib import ExitStack

import numpy as np

import concourse.bass as bass
from concourse import mybir
from concourse.alu_op_type import AluOpType as ALU

F32 = mybir.dt.float32
F32R = mybir.dt.float32r
I32 = mybir.dt.int32
ACT = mybir.ActivationFunctionType
AX = mybir.AxisListType.X

PART = 128
D = 1024
S = 256
TILES = S // PART
KT = D // PART
EPS = 1e-6
NEG = -1e30
DEPTH = 2
GW = D // 4
D_IN = 3488
D_IN2 = 2048
D_FF = 2816
D_FFE = 3584
EXPERTS = 8
HEADS = 8
MLA_HEADS, MLA_QK, MLA_NOPE, MLA_ROPE = 4, 96, 64, 32
HD = 64

COLS = {}
_at = 0
for _name, _n in (("cq", 256), ("ckv", 128), ("kr", 32), ("g_a", GW), ("c_h", GW), ("c_b", GW), ("c_c", GW),
                  ("g_b", GW), ("sg_u", GW), ("sg_v", GW), ("g_c", GW), ("mq", GW), ("mk", GW), ("mv", GW),
                  ("g_d", GW)):
    COLS[_name] = (_at, _at + _n)
    _at += _n

GAIN_ROWS = (("norm_g", 2, 8), ("mla_q_norm_g", 2, 2), ("mla_kv_norm_g", 2, 1), ("sg_b", 2, 4),
             ("norm_mix_2", 2, 8), ("pool_scale_2", 2, 4), ("attn_gain_2", 2, 4), ("norm_ffn_2", 2, 8))
GAIN_AT = {}
_at = 0
for _name, _l, _n in GAIN_ROWS:
    GAIN_AT[_name] = (_at, _n)
    _at += _l * _n
N_GAIN = _at

BCAST = {}
_at = 0
for _name, _n in (("mla_q_g", 96), ("mla_k_nope_g", 64), ("mla_k_rope_g", 32), ("moba_q_g", 64),
                  ("moba_k_g", 64), ("sg_ln_g", 256), ("sg_ln_b", 256), ("conv_w", 768)):
    BCAST[_name] = (_at, _at + _n)
    _at += _n
N_BCAST = _at

CONST = {}
_at = 0
for _name, _n in (("ident", 128), ("causal", 384), ("dilated", 384), ("inv", 16), ("shift", 4 * 128),
                  ("pool", 4 * 3 * 128), ("before", 128), ("ones", 128), ("upto", 128), ("iota", 128),
                  ("earlier", 64)):
    CONST[_name] = (_at, _at + _n)
    _at += _n
N_CONST = _at


def shape_constants():
    c = np.zeros((PART, N_CONST), np.float32)
    p = np.arange(PART)

    def put(name, a):
        c[:, CONST[name][0]:CONST[name][1]] = np.asarray(a, np.float32).reshape(PART, -1)

    put("ident", np.eye(PART))
    q0, q1, k = p[:, None], p[:, None] + PART, np.arange(S)[None, :]
    put("causal", np.concatenate([np.where(k[:, :PART] <= q0, 0.0, NEG), np.where(k <= q1, 0.0, NEG)], 1))
    def count(q, k):
        d = q - k
        n = (d >= 0) * ((d <= 128) * 1 + (d % 4 == 0) * (d <= 512) + (d % 16 == 0) * (d <= 2048))
        return np.where(n > 0, np.log(np.maximum(n, 1)) * HD ** 0.5, NEG)
    put("dilated", np.concatenate([count(q0, k[:, :PART]), count(q1, k)], 1))
    inv = 500000.0 ** (-np.arange(16, dtype=np.float64) * 2.0 / 32)
    put("inv", np.broadcast_to(inv.astype(np.float32), (PART, 16)))
    s, t = p[:, None], p[None, :]
    put("shift", np.stack([s == t - 1, s == t - 1 + PART, s == t - 2, s == t - 2 + PART], 1))
    m = []
    for w in (2, 4, 8, 16):
        ss, tt = np.arange(S)[:, None], np.arange(S)[None, :]
        full = np.where((ss <= tt) & (ss > tt - w), 1.0 / np.minimum(tt + 1, w), 0.0) - (ss == tt)
        m += [full[:PART, :PART], full[:PART, PART:], full[PART:, PART:]]
    put("pool", np.stack(m, 1))
    put("before", s < t)
    put("ones", np.ones((PART, PART)))
    put("upto", s <= t)
    put("iota", np.broadcast_to(p[None, :], (PART, PART)))
    e = np.arange(8)
    put("earlier", np.broadcast_to((e[None, :] < e[:, None]).reshape(1, 64), (PART, 64)))
    return c


RAW = 6
SPLIT = 3
KC = 4
NC = 512


def column_chunks(width):
    return [(n, min(NC, width - n), k, KC) for n in range(0, width, NC) for k in range(0, KT, KC)]


def row_chunks(rows):
    return [(n, NC, k, min(KC, rows // PART - k)) for k in range(0, rows // PART, KC) for n in (0, NC)]


HYBRID = [("in",) + c for c in column_chunks(D_IN)] + [("out",) + c for c in column_chunks(D)]
MIXER = [("in",) + c for c in column_chunks(D_IN2)] + [("out",) + c for c in column_chunks(D)]


def swiglu_chunks(width):
    cols = column_chunks(width)
    up = []
    for j in range(0, len(cols), 2):
        up += [("g",) + cols[j], ("g",) + cols[j + 1], ("u",) + cols[j], ("u",) + cols[j + 1]]
    return up, [("d",) + c for c in row_chunks(width)]


FFN_UP, FFN_DOWN = swiglu_chunks(D_FF)
MOE_UP, MOE_DOWN = swiglu_chunks(D_FFE)
FFN = FFN_UP + FFN_DOWN
MOE = MOE_UP + MOE_DOWN
AT_HYBRID = 0
AT_MIX0 = AT_HYBRID + DEPTH * len(HYBRID)
AT_FFN = AT_MIX0 + len(MIXER)
AT_MIX1 = AT_FFN + len(FFN)
AT_MOE = AT_MIX1 + len(MIXER)
BACK_AT = len(MOE_UP) + 4
GATHER_AT = len(MOE_UP) + 9
assert all(n % RAW == 0 for n in (len(HYBRID), AT_MIX0, AT_FFN, AT_MIX1, AT_MOE, len(MOE)))


def build(nc, A):
    ctx = ExitStack()
    with ctx:
        def sb(name, shape, dt=F32, stack=ctx):
            name = f"{name}_sb"
            return stack.enter_context(nc.sbuf_tensor(name, shape, dt))

        def sem(name):
            return ctx.enter_context(nc.semaphore(name))

        raw = [sb(f"raw{i}", [PART, KC, NC]) for i in range(RAW)]
        whi = [sb(f"whi{i}", [PART, KC, NC], F32R) for i in range(SPLIT)]
        wlo = [sb(f"wlo{i}", [PART, KC, NC], F32R) for i in range(SPLIT)]
        x = sb("x", [PART, TILES, D])
        xs = sb("xs", [PART, TILES, D])
        xT = sb("xT", [PART, KT, S])
        xhi = sb("xhi", [PART, KT, S], F32R)
        xlo = sb("xlo", [PART, KT, S], F32R)
        con = sb("con", [PART, N_CONST])
        gain = sb("gain", [PART, N_GAIN])
        pos = sb("pos", [PART, TILES], I32)
        trig = sb("trig", [PART, 2, TILES, 16])
        stat = sb("stat", [PART, 24])
        rs = sb("rs", [PART, 24])
        rs_tmp = sb("rs_tmp", [PART, 24])
        negm = sb("negm", [PART, HEADS, TILES])
        den = sb("den", [PART, HEADS, TILES])
        rden = sb("rden", [PART, HEADS, TILES])

        mixed = ExitStack()
        P = sb("P", [PART, TILES, D_IN], stack=mixed)
        QT = sb("QT", [PART, 6, S], stack=mixed)
        KTr = sb("KTr", [PART, 6, S], stack=mixed)
        T = sb("T", [PART, 1024], stack=mixed)
        w_uq = sb("w_uq", [PART, 2, 384], stack=mixed)
        w_ukv = sb("w_ukv", [PART, 512], stack=mixed)
        sgw = sb("sgw", [PART, 4, 128], stack=mixed)
        bc = sb("bc", [PART, N_BCAST], stack=mixed)
        mixed.close()
        swi = ExitStack()
        sg = sb("sg", [PART, TILES, NC], stack=swi)
        actv = sb("actv", [PART, TILES, NC], stack=swi)
        ahi = sb("ahi", [PART, D_FF // PART * S], F32R, stack=swi)
        alo = sb("alo", [PART, D_FF // PART * S], F32R, stack=swi)
        swi.close()
        moe = ExitStack()
        sg2 = sb("sg2", [PART, 1, NC], stack=moe)
        actv2 = sb("actv2", [PART, 1, NC], stack=moe)
        ahi2 = sb("ahi2", [PART, D_FFE], F32R, stack=moe)
        alo2 = sb("alo2", [PART, D_FFE], F32R, stack=moe)
        yg = sb("yg", [PART, D], stack=moe)
        pick = sb("pick", [PART, TILES, PART], stack=moe)
        pickg = sb("pickg", [PART, TILES, PART], stack=moe)
        backT = sb("backT", [PART, TILES, PART], stack=moe)
        w_rt = sb("w_rt", [PART, KT, EXPERTS], stack=moe)
        lg = sb("lg", [PART, TILES, EXPERTS], stack=moe)
        big = sb("big", [PART, TILES, 64], stack=moe)
        big2 = sb("big2", [PART, TILES, 64], stack=moe)
        rank = sb("rank", [PART, TILES, EXPERTS], stack=moe)
        sel = sb("sel", [PART, TILES, EXPERTS], stack=moe)
        gate = sb("gate", [PART, TILES, 2 * EXPERTS], stack=moe)
        slot = sb("slot", [PART, TILES, 2 * EXPERTS], stack=moe)
        small = sb("small", [PART, 8], stack=moe)
        over = sb("over", [PART, EXPERTS], stack=moe)
        overc = sb("overc", [PART, EXPERTS + 2], stack=moe)
        jobs_f = sb("jobs_f", [PART, 2 * EXPERTS + 1], stack=moe)
        jobs = sb("jobs", [1, 2 * EXPERTS + 1], I32, stack=moe)
        fin_g = sb("fin_g", [PART, D], stack=moe)
        moe.close()
        g_rows = raw[RAW - 1][0:N_GAIN, 0, 0:PART]

        ps = ctx.enter_context(nc.psum_tensor("ps", [PART, 8, NC], F32))
        acc = ps[:, 0:4, :].rearrange("p (a t) n -> p a t n", a=2)
        tp = ps[:, 4:8, :]

        raw_landed = [sem(f"raw_landed{i}") for i in range(RAW)]
        hi_ready = sem("hi_ready")
        lo_ready = sem("lo_ready")
        split_used = sem("split_used")
        acc_free = [sem(f"acc_free{i}") for i in range(2)]
        const_landed = sem("const_landed")
        rows_landed = sem("rows_landed")
        x_landed = sem("x_landed")
        small_landed = sem("small_landed")
        gain_ps = sem("gain_ps")
        gain_ready = sem("gain_ready")
        angle_ready = sem("angle_ready")
        trig_ready = sem("trig_ready")
        xs_ready = sem("xs_ready")
        xt_ps = sem("xt_ps")
        xt_f = sem("xt_f")
        xt_hi = sem("xt_hi")
        xt_lo = sem("xt_lo")
        gates_ready = sem("gates_ready")
        cn_ready = sem("cn_ready")
        cT_ps = sem("cT_ps")
        cT_ready = sem("cT_ready")
        sgT_ps = sem("sgT_ps")
        sgT_ready = sem("sgT_ready")
        zv_ready = sem("zv_ready")
        qkv_ps = sem("qkv_ps")
        conv_ps = sem("conv_ps")
        mix_ps = sem("mix_ps")
        sq_ready = sem("sq_ready")
        v_ready = sem("v_ready")
        qk_ready = sem("qk_ready")
        qT_ps = sem("qT_ps")
        qT_ready = sem("qT_ready")
        s_ps = sem("s_ps")
        s_masked = sem("s_masked")
        p_ready = sem("p_ready")
        pT_ps = sem("pT_ps")
        pT_ready = sem("pT_ready")
        o_ps = sem("o_ps")
        o_ready = sem("o_ready")
        layer_done = sem("layer_done")
        dT_ps = sem("dT_ps")
        dT_ready = sem("dT_ready")
        z_ps = sem("z_ps")
        act_ready = sem("act_ready")
        aT_ps = sem("aT_ps")
        ahi_ready = sem("ahi_ready")
        aT_ready = sem("aT_ready")
        lg_ps = sem("lg_ps")
        expl_ready = sem("expl_ready")
        lg_ready = sem("lg_ready")
        sel_ready = sem("sel_ready")
        cnt_ps = sem("cnt_ps")
        jobs_ready = sem("jobs_ready")
        pick_ready = sem("pick_ready")
        back_ps = sem("back_ps")
        xg_ps = sem("xg_ps")
        xg_f = sem("xg_f")
        xg_hi = sem("xg_hi")
        xg_lo = sem("xg_lo")
        back_ready = sem("back_ready")
        scat_ps = sem("scat_ps")
        scat_used = sem("scat_used")
        y_ready = sem("y_ready")
        out_written = sem("out_written")

        def C(name):
            a, b = CONST[name]
            return con[:, a:b]

        ident = C("ident")
        shift = C("shift").rearrange("p (j t) -> p j t", j=4)
        poolm = C("pool").rearrange("p (g j t) -> p g j t", g=4, j=3)

        def G(name, l):
            a, n = GAIN_AT[name]
            return gain[:, a + l * n:a + (l + 1) * n]

        def Gl(name, l):
            a, n = GAIN_AT[name]
            return gain[:, bass.ds(a + l * n, n)]

        def B(name):
            a, b = BCAST[name]
            return bc[:, a:b]

        def seg(name):
            a, b = COLS[name]
            return P[:, :, a:b]

        y = xs
        xT_flat = xT[:, :, :].rearrange("p a b -> p (a b)")
        qn = xT_flat[:, 0:768].rearrange("p (t h n) -> p t h n", t=TILES, h=MLA_HEADS)
        sgT = xT_flat[:, 768:1280].rearrange("p (g n) -> p g n", g=4)
        sm = xT_flat[:, 0:768].rearrange("p (r n) -> p r n", r=2)
        pr = xT_flat[:, 768:1536].rearrange("p (r n) -> p r n", r=2)
        pT = xT_flat[:, 1536:1920]
        krr = T[:, 0:64].rearrange("p (t n) -> p t n", t=TILES)
        rt = T[:, 64:64 + 4 * 128].rearrange("p (j n) -> p j n", j=4)
        cT = T[:, 0:768].rearrange("p (c n) -> p c n", c=3)
        kc = P[:, :, 0:384].rearrange("p t (h n) -> p t h n", h=MLA_HEADS)
        va = seg("c_c")

        def number(c0, i, per=0, l=0):
            return c0 + i + per * l

        def landed(c0, i, per=0, l=0):
            return 16 * (c0 // RAW + i // RAW + 1) + 16 * (per // RAW) * l

        def sp_chunk(sp, src, c0, i, shape, per=0, l=0):
            n0, n, k0, k = shape
            if i >= RAW or not isinstance(l, int) or c0 + per * l > 0:
                if isinstance(l, int) or i >= RAW or c0 >= RAW:
                    sp.wait_ge(lo_ready, number(c0, i - RAW + 1, per, l))
            sp.dma_start(raw[i % RAW][:, 0:k, 0:n],
                         src(k0 * PART, k * PART, n0, n)).then_inc(raw_landed[i % RAW], 16)

        def rows(w, l):
            def cut(r0, r, n0, n):
                if isinstance(l, int):
                    return w[l, r0:r0 + r, n0:n0 + n].rearrange("(c p) n -> p c n", p=PART)
                return w[bass.ds(l, 1), r0:r0 + r, n0:n0 + n].rearrange("a (c p) n -> p (a c) n", p=PART)
            return cut

        def sp_part(sp, chunks, srcs, c0, per=0, l=0):
            for i, (which, *shape) in enumerate(chunks):
                sp_chunk(sp, srcs[which], c0, i, shape, per, l)

        def sync_program(sp):
            hybrid0 = {"in": rows(A["w_in"], 0), "out": rows(A["w_out"], 0)}
            for i, (which, *shape) in enumerate(HYBRID):
                if i == RAW - 1:
                    sp.wait_ge(gain_ps, 1)
                sp_chunk(sp, hybrid0[which], AT_HYBRID, i, shape)
            with sp.Fori(1, DEPTH) as l:
                sp_part(sp, HYBRID, {"in": rows(A["w_in"], l), "out": rows(A["w_out"], l)},
                        AT_HYBRID + len(HYBRID), len(HYBRID), l - 1)
            for m, at in ((0, AT_MIX0), (1, AT_MIX1)):
                sp_part(sp, MIXER, {"in": rows(A["w_in_2"], m), "out": rows(A["w_out_2"], m)}, at)
                if m == 0:
                    sp_part(sp, FFN, {"g": rows(A["ffn_wg_2"], 0), "u": rows(A["ffn_wu_2"], 0),
                                      "d": rows(A["ffn_wd_2"], 0)}, AT_FFN)

            def expert(j, e):
                sp_part(sp, MOE, {"g": rows(wg, e), "u": rows(wu, e), "d": rows(wd, e)},
                        AT_MOE, len(MOE), j)

            wg, wu, wd = (A[n].rearrange("a e k n -> (a e) k n") for n in ("moe_wg_2", "moe_wu_2", "moe_wd_2"))
            with sp.Fori(0, EXPERTS) as j:
                expert(j, j)
            sp.wait_ge(jobs_ready, 1)
            n_jobs = sp.value_load(jobs[0:1, 2 * EXPERTS:2 * EXPERTS + 1], min_val=EXPERTS, max_val=2 * EXPERTS)
            with sp.If(n_jobs > EXPERTS):
                with sp.Fori(EXPERTS, n_jobs) as j:
                    e = sp.value_load(jobs[0:1, bass.ds(j, 1)], min_val=0, max_val=EXPERTS - 1)
                    expert(j, e)
            with sp.Else():
                sp.nop()
            for i in range(SPLIT):
                _, *shape = MOE[i]
                sp_chunk(sp, rows(wg, 0), AT_MOE, i, shape, len(MOE), n_jobs)
            sp.wait_ge(y_ready, 1)
            sp.dma_start(A["out"].rearrange("b (t p) d -> p (b t) d", p=PART), y[:, :, :]).then_inc(out_written, 16)
            sp.wait_ge(out_written, 16)

        N_SMALL = 11

        def pool_program(pool):
            pool.dma_start(con[:, :], A["consts"]).then_inc(const_landed, 16)
            pool.dma_start(pos[:, :], A["positions"].rearrange("b (t p) -> p (b t)", p=PART),
                           allow_slow_non_contiguous=True).then_inc(const_landed, 16)
            for name, n_l, n in GAIN_ROWS:
                a = GAIN_AT[name][0]
                src = A[name]
                if name == "sg_b":
                    src = src.rearrange("l g t -> (l g) t")
                else:
                    src = src.rearrange("l (c p) -> (l c) p", p=PART)
                pool.dma_start(raw[RAW - 1][a:a + n_l * n, 0, 0:PART], src).then_inc(rows_landed, 16)
            with pool.Fori(0, DEPTH) as l:
                pool.wait_ge(layer_done, l)
                pool.dma_start(w_uq[:, :, :], A["mla_w_uq"][bass.ds(l, 1), :, :].rearrange(
                    "a (c p) n -> p (a c) n", p=PART)).then_inc(small_landed, 16)
                pool.dma_start(w_ukv[:, :], A["mla_w_ukv"][bass.ds(l, 1), :, :].rearrange(
                    "a p n -> p (a n)")).then_inc(small_landed, 16)
                pool.dma_start(sgw[:, :, :], A["sg_w"][bass.ds(l, 1), :, :, :].rearrange(
                    "a g t s -> t (a g) s")).then_inc(small_landed, 16)
                for name, (a, b) in BCAST.items():
                    src = A[name]
                    if name == "conv_w":
                        src = src.rearrange("l w c -> l (w c)")
                    src = src[bass.ds(l, 1), :]
                    pool.dma_start(bc[:, a:b], src.to_broadcast([PART, b - a])).then_inc(small_landed, 16)
            for m in range(2):
                pool.wait_ge(layer_done, DEPTH + 2 * m)
                pool.dma_start(sgw[:, :, :], A["w_pool_2"][m].rearrange("g c e -> c g e")).then_inc(small_landed, 16)
            pool.wait_ge(layer_done, DEPTH + 3)
            pool.dma_start(w_rt[:, :, :], A["w_router_2"].rearrange("a (c p) e -> p (a c) e", p=PART)).then_inc(small_landed, 16)
            pool.dma_start(fin_g[:, :], A["final_norm_2"].rearrange("(a d) -> a d", a=1).to_broadcast(
                [PART, D])).then_inc(small_landed, 16)

        def small_at(layers, extra=0):
            return 16 * N_SMALL * layers + 16 * extra

        def act_hi(act, chunks, c0, i, per=0, l=0):
            _, _, n, _, k = chunks[i % len(chunks)]
            act.wait_ge(raw_landed[i % RAW], landed(c0, i, per, l))
            if not (isinstance(l, int) and c0 + i + per * l < SPLIT):
                act.wait_ge(split_used, number(c0, i - SPLIT + 1, per, l))
            for c in range(0, k, k // 2):
                nc.scalar.activation(whi[i % SPLIT][:, c:c + k // 2, 0:n], raw[i % RAW][:, c:c + k // 2, 0:n],
                                     ACT.Copy).then_inc(hi_ready, 1)

        def act_hiT(act, nT, with_gain):
            for h in range(2):
                if with_gain:
                    act.wait_ge(xt_f, 2 * nT[0] + h + 1)
                    src = xT[:, 4 * h:4 * h + 4, :]
                else:
                    act.wait_ge(xt_ps, 2 * nT[1] + h + 1)
                    src = tp[:, 2 * h:2 * h + 2, :].rearrange("p b (c n) -> p (b c) n", c=2)
                nc.scalar.activation(xhi[:, 4 * h:4 * h + 4, :], src, ACT.Copy).then_inc(xt_hi, 1)

        def act_attention(act, att, scales):
            def exps(h):
                act.wait_ge(s_masked, HEADS * att + h + 1)
                if h >= 2:
                    act.wait_ge(pT_ps, HEADS * att + h - 1)
                r = h % 2
                nc.scalar.activation(pr[:, r, 0:128], sm[:, r, 0:128], ACT.Exp, bias=negm[:, h, 0:1],
                                     scale=scales[h], accum_out=den[:, h, 0:1])
                nc.scalar.activation(pr[:, r, 128:384], sm[:, r, 128:384], ACT.Exp, bias=negm[:, h, 1:2],
                                     scale=scales[h], accum_out=den[:, h, 1:2]).then_inc(p_ready, 1)

            def copy(h):
                act.wait_ge(pT_ps, HEADS * att + h + 1)
                if h >= 1:
                    act.wait_ge(o_ps, HEADS * att + h)
                nc.scalar.activation(pT, tp[:, 2 + h % 2, 0:384], ACT.Copy).then_inc(pT_ready, 1)

            exps(0)
            for h in range(HEADS):
                if h + 1 < HEADS:
                    exps(h + 1)
                copy(h)

        def copy_proj(act, g, width, used):
            n0 = g * NC
            n = min(NC, width - n0)
            act.wait_ge(split_used, used)
            nc.scalar.activation(P[:, :, n0:n0 + n], acc[:, g % 2, :, 0:n], ACT.Copy).then_inc(acc_free[g % 2], 1)

        def scalar_program(act):
            act.wait_ge(angle_ready, 1)
            nc.scalar.activation(trig[:, :, :, :], T[:, 0:64].rearrange("p (a t n) -> p a t n", a=2, t=TILES),
                                 ACT.Sin).then_inc(trig_ready, 1)
            for i in range(SPLIT):
                act_hi(act, HYBRID, AT_HYBRID, i)
            n_in = len(column_chunks(D_IN))
            with act.Fori(0, DEPTH) as l:
                act_hiT(act, (l, None), True)
                for i in range(n_in):
                    act_hi(act, HYBRID, AT_HYBRID, i + SPLIT, len(HYBRID), l)
                    if i % 2:
                        copy_proj(act, i // 2, D_IN, number(AT_HYBRID, i + 1, len(HYBRID), l))
                act.drain()
                for name in ("g_a", "g_b", "g_c", "g_d"):
                    last = nc.scalar.activation(seg(name), seg(name), ACT.Silu)
                last.then_inc(gates_ready, 1)
                act.wait_ge(qkv_ps, l + 1)
                nc.scalar.activation(xs[:, :, 0:384], acc[:, 1, :, 0:384], ACT.Square)
                kv_ps = tp[:, 0:2, :].rearrange("p t (h n) -> p t h n", h=MLA_HEADS)
                for t in range(TILES):
                    last = nc.scalar.activation(xs[:, t, 384:640].rearrange("p (h n) -> p h n", h=MLA_HEADS),
                                                kv_ps[:, t, :, 0:64], ACT.Square)
                last.then_inc(sq_ready, 1)
                for t in range(TILES):
                    last = nc.scalar.activation(va[:, t, :].rearrange("p (h n) -> p h n", h=MLA_HEADS),
                                                kv_ps[:, t, :, 64:128], ACT.Copy)
                last.then_inc(v_ready, 1)
                act.wait_ge(qT_ps, 4 * l + 1)
                nc.scalar.activation(QT[0:96, 0:4, :], ps[0:96, 2:4, :].rearrange("p b (c n) -> p (b c) n", c=2),
                                     ACT.Copy).then_inc(qT_ready, 1)
                act.wait_ge(qT_ps, 4 * l + 2)
                nc.scalar.activation(KTr[0:96, 0:4, :], tp[0:96, 0:2, :].rearrange("p b (c n) -> p (b c) n", c=2),
                                     ACT.Copy).then_inc(qT_ready, 1)
                act.wait_ge(qT_ps, 4 * l + 3)
                nc.scalar.activation(QT[:, 4:6, :], tp[:, 2, :].rearrange("p (c n) -> p c n", c=2),
                                     ACT.Copy).then_inc(qT_ready, 1)
                act.wait_ge(qT_ps, 4 * l + 4)
                nc.scalar.activation(KTr[:, 4:6, :], ps[:, 2, :].rearrange("p (c n) -> p c n", c=2),
                                     ACT.Copy).then_inc(qT_ready, 1)
                act_attention(act, l, [MLA_QK ** -0.5] * 4 + [HD ** -0.5] * 4)
                act_hiT(act, (None, 2 * l + 1), False)
                for i in range(n_in, len(HYBRID)):
                    act_hi(act, HYBRID, AT_HYBRID, i + SPLIT, len(HYBRID), l)

            def mixer(m, at, accr):
                act_hiT(act, (DEPTH + 3 * m, None), True)
                n_in = len(column_chunks(D_IN2))
                for i in range(n_in):
                    act_hi(act, MIXER, at, i + SPLIT)
                    if i % 2:
                        copy_proj(act, i // 2, D_IN2, number(at, i + 1))
                q = 4 * DEPTH + 2 * m
                act.wait_ge(qT_ps, q + 1)
                nc.scalar.activation(QT[:, 0:4, :], tp[:, 0:2, :].rearrange("p b (c n) -> p (b c) n", c=2),
                                     ACT.Copy).then_inc(qT_ready, 1)
                act.wait_ge(qT_ps, q + 2)
                nc.scalar.activation(KTr[:, 0:4, :], tp[:, 2:4, :].rearrange("p b (c n) -> p (b c) n", c=2),
                                     ACT.Copy).then_inc(qT_ready, 1)
                act.wait_ge(dT_ps, m + 1)
                nc.scalar.activation(T[:, :], ps[:, 0:2, :].rearrange("p b n -> p (b n)"), ACT.Copy).then_inc(dT_ready, 1)
                act_attention(act, DEPTH + m, [HD ** -0.5] * HEADS)
                act_hiT(act, (DEPTH + 3 * m + 1, None), True)
                for i in range(n_in, len(MIXER)):
                    if m == 0:
                        act_hi(act, MIXER, at, i + SPLIT)
                    elif i + SPLIT < len(MIXER):
                        act_hi(act, MIXER, at, i + SPLIT)

            def swiglu(chunks, n_up, at, tiles, sgb, hib, ups, jobsn, per=0, l=0, ahead=False, between=None):
                for i in range(len(chunks)):
                    if i + SPLIT < len(chunks) or ahead:
                        act_hi(act, chunks, at, i + SPLIT, per, l)
                    if i < n_up and i % 4 == 2:
                        j = i // 4
                        n = chunks[i][2]
                        act.wait_ge(split_used, number(at, i, per, l))
                        act.wait_ge(act_ready, jobsn + j)
                        nc.scalar.activation(sgb[:, 0:tiles, 0:n], acc[:, 0, 0:tiles, 0:n], ACT.Silu).then_inc(acc_free[0], 1)
                    if i >= 6 and (i - 6) % 4 == 0 and (i - 6) // 4 < ups:
                        j = (i - 6) // 4
                        nb = chunks[4 * j][2] // PART
                        act.wait_ge(aT_ps, jobsn + j + 1)
                        w = tiles * PART
                        src = tp[:, 2 * (j % 2):2 * (j % 2) + tiles, :].rearrange("p b n -> p (b n)")[:, 0:nb * w]
                        nc.scalar.activation(hib[:, 4 * j * w:4 * j * w + nb * w], src, ACT.Copy).then_inc(ahi_ready, 1)
                    if between:
                        between(i)

            mixer(0, AT_MIX0, 18)
            act_hiT(act, (DEPTH + 2, None), True)
            swiglu(FFN, len(FFN_UP), AT_FFN, TILES, sg, ahi, 6, 0, ahead=True)
            mixer(1, AT_MIX1, 38)
            for i in range(SPLIT):
                act_hi(act, MOE, AT_MOE, i)
            act.wait_ge(lg_ready, 1)
            nc.scalar.activation(lg[:, :, :], lg[:, :, :], ACT.Exp).then_inc(expl_ready, 1)
            act.wait_ge(jobs_ready, 1)
            n_jobs = act.value_load(jobs[0:1, 2 * EXPERTS:2 * EXPERTS + 1], min_val=EXPERTS, max_val=2 * EXPERTS)

            def gathered(job):
                act.wait_ge(xg_f, job + 1)
                nc.scalar.activation(xhi[:, :, 0:PART], xT[:, :, 0:PART], ACT.Copy).then_inc(xg_hi, 1)

            gathered(0)
            with act.Fori(0, n_jobs) as j:

                def between(i):
                    if i == BACK_AT:
                        act.wait_ge(back_ps, j + 1)
                        nc.scalar.activation(backT[:, :, :], tp[:, 2, 0:256].rearrange("p (t n) -> p t n", t=TILES),
                                             ACT.Copy).then_inc(back_ready, 1)
                    if i == GATHER_AT:
                        gathered(j + 1)

                swiglu(MOE, len(MOE_UP), AT_MOE, 1, sg2, ahi2, 7, 6 + 7 * j, len(MOE), j, ahead=True, between=between)
                for n in range(2):
                    act.wait_ge(split_used, number(AT_MOE, len(MOE) - 1 + n, len(MOE), j))
                    nc.scalar.activation(yg[:, n * NC:(n + 1) * NC], acc[:, n, 0, :], ACT.Copy).then_inc(acc_free[n], 1)

        V = nc.vector

        def dve_lo(dve, chunks, c0, i, per=0, l=0):
            _, _, n, _, k = chunks[i % len(chunks)]
            for c in range(0, k, k // 2):
                dve.wait_ge(hi_ready, 2 * c0 + 2 * i + (2 if c else 1) + 2 * per * l)
                op = V.tensor_tensor(wlo[i % SPLIT][:, c:c + k // 2, 0:n], raw[i % RAW][:, c:c + k // 2, 0:n],
                                     whi[i % SPLIT][:, c:c + k // 2, 0:n], ALU.subtract)
            op.then_inc(lo_ready, 1)

        def rsqrt(dve, v, out, tmp):
            V.tensor_scalar(out.bitcast(I32), v.bitcast(I32), 1, None, ALU.logical_shift_right)
            dve.drain()
            V.tensor_scalar(out.bitcast(I32), out.bitcast(I32), -1.0, float(0x5f3759df), ALU.mult, ALU.add)
            for _ in range(4):
                dve.drain()
                V.tensor_tensor(tmp, out, out, ALU.mult)
                dve.drain()
                V.scalar_tensor_tensor(out=tmp, in0=tmp, scalar=-0.5, in1=v, op0=ALU.mult, op1=ALU.mult)
                dve.drain()
                V.scalar_tensor_tensor(out=out, in0=tmp, scalar=1.5, in1=out, op0=ALU.add, op1=ALU.mult)
            dve.drain()

        def norm_rows(dve, src, width, out, acol=0):
            for t in range(TILES):
                V.tensor_tensor_reduce(out=out[:, t, :], in0=src[:, t, :], in1=src[:, t, :], scale=1.0 / width,
                                       scalar=EPS, op0=ALU.mult, op1=ALU.add, accum_out=stat[:, t:t + 1])
            dve.drain()
            rsqrt(dve, stat[:, 0:2], rs[:, 0:2], rs_tmp[:, 0:2])
            for t in range(TILES):
                last = V.tensor_scalar(out[:, t, :], src[:, t, :], rs[:, t:t + 1], None, ALU.mult)
            return last

        def dve_T(dve, nT, nF, g):
            for h in range(2):
                dve.wait_ge(xt_ps, 2 * nT + h + 1)
                if g is not None:
                    V.tensor_tensor(xT[:, 4 * h:4 * h + 4, :],
                                    tp[:, 2 * h:2 * h + 2, :].rearrange("p b (c n) -> p (b c) n", c=2),
                                    g(h).unsqueeze(2).to_broadcast([PART, 4, S]), ALU.mult).then_inc(xt_f, 1)
            for h in range(2):
                dve.wait_ge(xt_hi, 2 * nT + h + 1)
                src = (xT[:, 4 * h:4 * h + 4, :] if g is not None else
                       tp[:, 2 * h:2 * h + 2, :].rearrange("p b (c n) -> p (b c) n", c=2))
                V.tensor_tensor(xlo[:, 4 * h:4 * h + 4, :], src, xhi[:, 4 * h:4 * h + 4, :],
                                ALU.subtract).then_inc(xt_lo, 1)

        def dve_attention(dve, att, mask, scales, at_col):
            def masked(h):
                r = h % 2
                dve.wait_ge(s_ps, HEADS * att + h + 1)
                if h >= 2:
                    dve.wait_ge(p_ready, HEADS * att + h - 1)
                V.tensor_tensor(sm[:, r, :], tp[:, r, 0:384], mask, ALU.add)
                dve.drain()
                V.tensor_reduce(negm[:, h, 0:1], sm[:, r, 0:128], AX, ALU.max)
                V.tensor_reduce(negm[:, h, 1:2], sm[:, r, 128:384], AX, ALU.max)
                dve.drain()
                V.tensor_scalar(negm[:, h, :], negm[:, h, :], -scales[h], None, ALU.mult).then_inc(s_masked, 1)

            def divide(h):
                dve.wait_ge(p_ready, HEADS * att + h + 1)
                V.reciprocal(rden[:, h, :], den[:, h, :])
                dve.drain()
                dve.wait_ge(o_ps, HEADS * att + h + 1)
                src = ps[:, h % 2, 0:2 * HD].rearrange("p (t n) -> p t n", t=TILES)
                at = at_col(h)
                V.tensor_tensor(y[:, :, at:at + HD], src, rden[:, h, :].unsqueeze(2).to_broadcast([PART, TILES, HD]),
                                ALU.mult).then_inc(o_ready, 1)

            masked(0)
            for h in range(HEADS):
                if h + 1 < HEADS:
                    masked(h + 1)
                divide(h)
            dve.drain()

        def rope(dve, v1, v2, o1, o2, heads, half, step):
            shp = [PART, TILES, heads, half]
            cs, sn = (trig[:, j, :, 0:16:step].unsqueeze(2).to_broadcast(shp) for j in range(2))
            n = TILES * heads * half
            t = [rt[:, j, 0:n].rearrange("p (t h n) -> p t h n", t=TILES, h=heads) for j in range(4)]
            V.tensor_tensor(t[0], v1, cs, ALU.mult)
            V.tensor_tensor(t[1], v2, sn, ALU.mult)
            V.tensor_tensor(t[2], v2, cs, ALU.mult)
            V.tensor_tensor(t[3], v1, sn, ALU.mult)
            dve.drain()
            V.tensor_tensor(o1, t[0], t[1], ALU.subtract)
            V.tensor_tensor(o2, t[2], t[3], ALU.add)
            dve.drain()

        def add_out(dve, chunks, n_in, c0, accr, free0, per=0, l=0, last_part=False):
            for i in range(n_in, len(chunks)):
                if not last_part or i + SPLIT < len(chunks):
                    dve_lo(dve, chunks, c0, i + SPLIT, per, l)
                if i % 2:
                    g = i // 2
                    n0 = (i - n_in) // 2 * NC
                    dve.wait_ge(split_used, number(c0, i + 1, per, l))
                    V.tensor_tensor(x[:, :, n0:n0 + NC], x[:, :, n0:n0 + NC], acc[:, g % 2, :, :],
                                    ALU.add).then_inc(acc_free[g % 2], 1)
            dve.drain()

        def vector_program(dve):
            dve.wait_ge(gain_ps, 1)
            V.tensor_copy(gain[:, :], tp[:, 0, 0:N_GAIN]).then_inc(gain_ready, 1)
            two_pi = 2 * np.pi
            parts = []
            rest = two_pi
            for _ in range(3):
                m = float(2.0 ** (np.floor(np.log2(rest)) - 7))
                parts.append(float(np.floor(rest / m) * m))
                rest -= parts[-1]
            parts.append(float(np.float32(rest)))
            ang = T[:, 0:64].rearrange("p (a t n) -> p a t n", a=2, t=TILES)
            turns = T[:, 64:96].rearrange("p (t n) -> p t n", t=TILES)
            posf = T[:, 96:98]
            V.tensor_copy(posf, pos[:, :])
            dve.drain()
            V.tensor_tensor(ang[:, 1], posf.unsqueeze(2).to_broadcast([PART, TILES, 16]),
                            C("inv").unsqueeze(1).to_broadcast([PART, TILES, 16]), ALU.mult)
            dve.drain()
            round_at = 1.5 * 2.0 ** 23
            V.tensor_scalar(turns, ang[:, 1], float(1.0 / two_pi), None, ALU.mult)
            dve.drain()
            V.tensor_scalar(turns, turns, round_at, None, ALU.add)
            dve.drain()
            V.tensor_scalar(turns, turns, -round_at, None, ALU.add)
            dve.drain()
            for part in parts:
                V.scalar_tensor_tensor(out=ang[:, 1], in0=turns, scalar=-part, in1=ang[:, 1], op0=ALU.mult, op1=ALU.add)
                dve.drain()
            V.tensor_scalar(ang[:, 0], ang[:, 1], float(np.pi / 2), None, ALU.add)
            dve.drain()
            V.tensor_scalar(turns, ang[:, 0], float(np.pi), -two_pi, ALU.is_gt, ALU.mult)
            dve.drain()
            V.tensor_tensor(ang[:, 0], ang[:, 0], turns, ALU.add)
            dve.drain()
            below = float(np.nextafter(np.float32(np.pi), np.float32(0)))
            V.tensor_scalar(T[:, 0:64], T[:, 0:64], below, -below, ALU.min, ALU.max).then_inc(angle_ready, 1)
            dve.wait_ge(x_landed, 16)
            for i in range(SPLIT):
                dve_lo(dve, HYBRID, AT_HYBRID, i)
            n_in = len(column_chunks(D_IN))
            dve.wait_ge(trig_ready, 1)
            with dve.Fori(0, DEPTH) as l:
                norm_rows(dve, x, D, xs).then_inc(xs_ready, 1)
                a_g, n_g = GAIN_AT["norm_g"]
                dve_T(dve, 2 * l, l, lambda h: gain[:, bass.ds(a_g + 4 * h + l * n_g, 4)])
                for i in range(n_in):
                    dve_lo(dve, HYBRID, AT_HYBRID, i + SPLIT, len(HYBRID), l)
                dve.wait_ge(acc_free[1], 4 * l + 3)
                dve.wait_ge(acc_free[0], 5 * l + 4)
                dve.wait_ge(small_landed, 16 * N_SMALL * (l + 1))
                sq = xs
                V.tensor_tensor(sq[:, :, 0:416], P[:, :, 0:416], P[:, :, 0:416], ALU.mult)
                mqk = P[:, :, COLS["mq"][0]:COLS["mk"][1]]
                V.tensor_tensor(sq[:, :, 416:928], mqk, mqk, ALU.mult)
                sgv = seg("sg_v")
                V.tensor_reduce(stat[:, 22:24], sgv, AX, ALU.add)
                dve.drain()
                V.tensor_reduce(stat[:, 0:2], sq[:, :, 0:256], AX, ALU.add)
                V.tensor_reduce(stat[:, 2:4], sq[:, :, 256:384], AX, ALU.add)
                V.tensor_reduce(stat[:, 4:6], sq[:, :, 384:416], AX, ALU.add)
                V.tensor_reduce(stat[:, 6:22].rearrange("p (t h) -> p t h", t=TILES),
                                sq[:, :, 416:928].rearrange("p t (h n) -> p t h n", h=8), AX, ALU.add)
                V.tensor_scalar(stat[:, 22:24], stat[:, 22:24], -1.0 / GW, None, ALU.mult)
                dve.drain()
                V.tensor_tensor(sgv, sgv, stat[:, 22:24].unsqueeze(2).to_broadcast([PART, TILES, GW]), ALU.add)
                dve.drain()
                V.tensor_tensor(sq[:, :, 0:256], sgv, sgv, ALU.mult)
                dve.drain()
                V.tensor_reduce(stat[:, 22:24], sq[:, :, 0:256], AX, ALU.add)
                dve.drain()
                for a, b, n in ((0, 2, 256), (2, 4, 128), (4, 6, 32), (6, 22, 64), (22, 24, 256)):
                    V.tensor_scalar(stat[:, a:b], stat[:, a:b], 1.0 / n, EPS, ALU.mult, ALU.add)
                dve.drain()
                rsqrt(dve, stat[:, :], rs[:, :], rs_tmp[:, :])
                V.tensor_tensor(seg("cq"), seg("cq"), rs[:, 0:2].unsqueeze(2).to_broadcast([PART, TILES, 256]), ALU.mult)
                V.tensor_tensor(seg("ckv"), seg("ckv"), rs[:, 2:4].unsqueeze(2).to_broadcast([PART, TILES, 128]),
                                ALU.mult).then_inc(cn_ready, 1)
                V.tensor_tensor(seg("c_h"), seg("c_h"), seg("c_c"), ALU.mult)
                V.tensor_tensor(sgv, sgv, rs[:, 22:24].unsqueeze(2).to_broadcast([PART, TILES, GW]), ALU.mult)
                dve.drain()
                V.tensor_tensor(sgv, sgv, B("sg_ln_g").unsqueeze(1).to_broadcast([PART, TILES, GW]), ALU.mult)
                dve.drain()
                V.tensor_tensor(sgv, sgv, B("sg_ln_b").unsqueeze(1).to_broadcast([PART, TILES, GW]),
                                ALU.add).then_inc(zv_ready, 1)
                dve.wait_ge(cT_ps, l + 1)
                a_q, a_kv = GAIN_AT["mla_q_norm_g"][0], GAIN_AT["mla_kv_norm_g"][0]
                V.tensor_tensor(cT[:, 0:2, :], tp[:, 0, :].rearrange("p (c n) -> p c n", c=2),
                                gain[:, bass.ds(a_q + l * 2, 2)].unsqueeze(2).to_broadcast([PART, 2, S]), ALU.mult)
                V.tensor_scalar(cT[:, 2, :], tp[:, 1, 0:S], gain[:, bass.ds(a_kv + l, 1)], None,
                                ALU.mult).then_inc(cT_ready, 1)
                dve.wait_ge(sgT_ps, l + 1)
                V.tensor_tensor(sgT, tp[:, 2, :].rearrange("p (g t) -> p g t", g=4),
                                C("upto").unsqueeze(1).to_broadcast([PART, 4, 128]), ALU.mult).then_inc(sgT_ready, 1)
                m4 = mqk.rearrange("p t (h n) -> p t h n", h=8)
                V.tensor_tensor(m4, m4, rs[:, 6:22].rearrange("p (t h) -> p t h", t=TILES).unsqueeze(3)
                                .to_broadcast([PART, TILES, 8, HD]), ALU.mult)
                dve.drain()
                for j, name in enumerate(("moba_q_g", "moba_k_g")):
                    V.tensor_tensor(m4[:, :, 4 * j:4 * j + 4, :], m4[:, :, 4 * j:4 * j + 4, :],
                                    B(name).unsqueeze(1).unsqueeze(1).to_broadcast([PART, TILES, 4, HD]), ALU.mult)
                dve.drain()
                dve.wait_ge(qkv_ps, l + 1)
                rope(dve, m4[:, :, :, 0:8], m4[:, :, :, 8:16], m4[:, :, :, 0:8], m4[:, :, :, 8:16], 8, 8, 2)
                kr = seg("kr")
                V.tensor_tensor(kr, kr, rs[:, 4:6].unsqueeze(2).to_broadcast([PART, TILES, 32]), ALU.mult)
                dve.drain()
                V.tensor_tensor(kr, kr, B("mla_k_rope_g").unsqueeze(1).to_broadcast([PART, TILES, 32]), ALU.mult)
                dve.drain()
                kr4, kro4 = kr.unsqueeze(2), krr.unsqueeze(2)
                rope(dve, kr4[:, :, :, 0:16], kr4[:, :, :, 16:32], kro4[:, :, :, 0:16], kro4[:, :, :, 16:32], 1, 16, 1)
                dve.wait_ge(sq_ready, l + 1)
                V.tensor_reduce(stat[:, 0:8].rearrange("p (t h) -> p t h", t=TILES),
                                xs[:, :, 0:384].rearrange("p t (h n) -> p t h n", h=4), AX, ALU.add)
                V.tensor_reduce(stat[:, 8:16].rearrange("p (t h) -> p t h", t=TILES),
                                xs[:, :, 384:640].rearrange("p t (h n) -> p t h n", h=4), AX, ALU.add)
                dve.drain()
                V.tensor_scalar(stat[:, 0:8], stat[:, 0:8], 1.0 / MLA_QK, EPS, ALU.mult, ALU.add)
                V.tensor_scalar(stat[:, 8:16], stat[:, 8:16], 1.0 / MLA_NOPE, EPS, ALU.mult, ALU.add)
                dve.drain()
                rsqrt(dve, stat[:, 0:16], rs[:, 0:16], rs_tmp[:, 0:16])
                kv_ps = tp[:, 0:2, :].rearrange("p t (h n) -> p t h n", h=MLA_HEADS)
                dve.wait_ge(v_ready, l + 1)
                V.tensor_tensor(qn, acc[:, 1, :, 0:384].rearrange("p t (h n) -> p t h n", h=4),
                                rs[:, 0:8].rearrange("p (t h) -> p t h", t=TILES).unsqueeze(3)
                                .to_broadcast([PART, TILES, 4, MLA_QK]), ALU.mult)
                V.tensor_tensor(kc[:, :, :, 0:64], kv_ps[:, :, :, 0:64],
                                rs[:, 8:16].rearrange("p (t h) -> p t h", t=TILES).unsqueeze(3)
                                .to_broadcast([PART, TILES, 4, 64]), ALU.mult)
                V.tensor_copy(kc[:, :, :, 64:96], krr.unsqueeze(2).to_broadcast([PART, TILES, 4, 32]))
                dve.drain()
                V.tensor_tensor(qn, qn, B("mla_q_g").unsqueeze(1).unsqueeze(1)
                                .to_broadcast([PART, TILES, 4, MLA_QK]), ALU.mult)
                V.tensor_tensor(kc[:, :, :, 0:64], kc[:, :, :, 0:64], B("mla_k_nope_g").unsqueeze(1).unsqueeze(1)
                                .to_broadcast([PART, TILES, 4, 64]), ALU.mult)
                dve.drain()
                rope(dve, qn[:, :, :, 64:80], qn[:, :, :, 80:96], qn[:, :, :, 64:80], qn[:, :, :, 80:96], 4, 16, 1)
                dve.sem_inc(qk_ready, 1)
                dve.wait_ge(conv_ps, l + 1)
                dve.wait_ge(gates_ready, l + 1)
                ob = y[:, :, 256:512]
                cw = B("conv_w").rearrange("p (w c) -> p w c", w=3)
                wof = [cw[:, j:j + 1, :].to_broadcast([PART, TILES, GW]) for j in range(3)]
                t_a = T[:, 0:512].rearrange("p (t n) -> p t n", t=TILES)
                V.tensor_tensor(ob, seg("c_h"), wof[2], ALU.mult)
                V.tensor_tensor(t_a, ps[:, 0, :].rearrange("p (t n) -> p t n", t=TILES), wof[1], ALU.mult)
                dve.drain()
                V.tensor_tensor(ob, ob, t_a, ALU.add)
                dve.drain()
                V.tensor_tensor(t_a, ps[:, 1, :].rearrange("p (t n) -> p t n", t=TILES), wof[0], ALU.mult)
                dve.drain()
                V.tensor_tensor(ob, ob, t_a, ALU.add)
                V.tensor_tensor(seg("c_b"), seg("c_b"), seg("g_b"), ALU.mult)
                dve.drain()
                V.tensor_tensor(ob, ob, seg("c_b"), ALU.mult)
                dve.wait_ge(mix_ps, l + 1)
                oc = y[:, :, 512:768]
                a_b = GAIN_AT["sg_b"][0]
                for t in range(TILES):
                    V.tensor_tensor(oc[:, t, :].rearrange("p (g n) -> p g n", g=4),
                                    tp[:, 3, t * 256:(t + 1) * 256].rearrange("p (g n) -> p g n", g=4),
                                    gain[:, bass.ds(a_b + l * 4, 4)].unsqueeze(2).to_broadcast([PART, 4, 64]), ALU.add)
                V.tensor_tensor(seg("sg_u"), seg("sg_u"), seg("g_c"), ALU.mult)
                dve.drain()
                V.tensor_tensor(oc, oc, seg("sg_u"), ALU.mult)
                dve_attention(dve, l, C("causal"), [MLA_QK ** -0.5] * 4 + [HD ** -0.5] * 4,
                              lambda h: h * HD if h < 4 else 768 + (h - 4) * HD)
                V.tensor_tensor(y[:, :, 0:256], y[:, :, 0:256], seg("g_a"), ALU.mult)
                V.tensor_tensor(y[:, :, 768:1024], y[:, :, 768:1024], seg("g_d"), ALU.mult)
                dve.drain()
                dve.sem_inc(xs_ready, 1)
                dve_T(dve, 2 * l + 1, None, None)
                add_out(dve, HYBRID, n_in, AT_HYBRID, 9 * l, None, len(HYBRID), l)
                dve.sem_inc(layer_done, 1)

            def mixer(m, at, accr):
                norm_rows(dve, x, D, xs).then_inc(xs_ready, 1)
                nT = 2 * DEPTH + 3 * m
                dve_T(dve, nT, None, lambda h: G("norm_mix_2", m)[:, 4 * h:4 * h + 4])
                n_in = len(column_chunks(D_IN2))
                for i in range(n_in):
                    dve_lo(dve, MIXER, at, i + SPLIT)
                dve.wait_ge(z_ps, m + 1)
                for t in range(TILES):
                    V.tensor_copy(y[:, t, 0:512], ps[:, 2 + t, :])
                dve.drain()
                norm_rows(dve, y[:, :, 0:512], 512, T[:, :].rearrange("p (t n) -> p t n", t=TILES))
                dve.drain()
                V.tensor_copy(y[:, :, 0:512], T[:, :].rearrange("p (t n) -> p t n", t=TILES))
                dve_attention(dve, DEPTH + m, C("dilated"), [HD ** -0.5] * HEADS, lambda h: 512 + h * HD)
                norm_rows(dve, y[:, :, 512:1024], 512, T[:, :].rearrange("p (t n) -> p t n", t=TILES))
                dve.drain()
                V.tensor_copy(y[:, :, 512:1024], T[:, :].rearrange("p (t n) -> p t n", t=TILES)).then_inc(xs_ready, 1)
                dve_T(dve, nT + 1, None, lambda h: G("attn_gain_2" if h else "pool_scale_2", m))
                add_out(dve, MIXER, n_in, at, accr, None, last_part=m == 1)
                dve.sem_inc(layer_done, 1)

            def swiglu(chunks, n_up, at, tiles, sgb, actb, hib, lob, ups, free0, jobsn, per=0, l=0, ahead=False, between=None):
                for i in range(len(chunks)):
                    if i + SPLIT < len(chunks) or ahead:
                        dve_lo(dve, chunks, at, i + SPLIT, per, l)
                    if i < n_up and i % 4 == 3:
                        j = i // 4
                        n = chunks[i][2]
                        dve.wait_ge(split_used, number(at, i + 1, per, l))
                        dve.wait_ge(acc_free[0], free0 + j + 1)
                        dve.wait_ge(aT_ps, jobsn + j)
                        V.tensor_tensor(actb[:, 0:tiles, 0:n], acc[:, 1, 0:tiles, 0:n], sgb[:, 0:tiles, 0:n],
                                        ALU.mult).then_inc(act_ready, 1)
                    if i >= 6 and (i - 6) % 4 == 0 and (i - 6) // 4 < ups:
                        j = (i - 6) // 4
                        nb = chunks[4 * j][2] // PART
                        w = tiles * PART
                        dve.wait_ge(ahi_ready, jobsn + j + 1)
                        src = tp[:, 2 * (j % 2):2 * (j % 2) + tiles, :].rearrange("p b n -> p (b n)")[:, 0:nb * w]
                        V.tensor_tensor(lob[:, 4 * j * w:4 * j * w + nb * w], src, hib[:, 4 * j * w:4 * j * w + nb * w],
                                        ALU.subtract).then_inc(aT_ready, 1)
                    if between:
                        between(i)

            mixer(0, AT_MIX0, 18)
            norm_rows(dve, x, D, xs).then_inc(xs_ready, 1)
            dve_T(dve, 2 * DEPTH + 2, None, lambda h: G("norm_ffn_2", 0)[:, 4 * h:4 * h + 4])
            swiglu(FFN, len(FFN_UP), AT_FFN, TILES, sg, actv, ahi, alo, 6, 13, 0, ahead=True)
            dve.wait_ge(split_used, AT_FFN + len(FFN))
            for n in range(2):
                V.tensor_tensor(x[:, :, n * NC:(n + 1) * NC], x[:, :, n * NC:(n + 1) * NC], acc[:, n, :, :],
                                ALU.add).then_inc(acc_free[n], 1)
            dve.drain()
            dve.sem_inc(layer_done, 1)
            mixer(1, AT_MIX1, 38)
            for i in range(SPLIT):
                dve_lo(dve, MOE, AT_MOE, i)
            norm_rows(dve, x, D, xs).then_inc(xs_ready, 1)
            g_ffn = G("norm_ffn_2", 1)
            for h in range(2):
                dve.wait_ge(xt_ps, 2 * (2 * DEPTH + 5) + h + 1)
                V.tensor_tensor(xT[:, 4 * h:4 * h + 4, :],
                                tp[:, 2 * h:2 * h + 2, :].rearrange("p b (c n) -> p (b c) n", c=2),
                                g_ffn[:, 4 * h:4 * h + 4].unsqueeze(2).to_broadcast([PART, 4, S]), ALU.mult).then_inc(xt_f, 1)
            dve.wait_ge(lg_ps, 1)
            V.tensor_copy(lg[:, :, :], ps[:, 0, 0:16].rearrange("p (t e) -> p t e", t=TILES))
            dve.drain()
            b4 = [PART, TILES, 8, 8]
            mine = lg[:, :, :].unsqueeze(3).to_broadcast(b4)
            other = lg[:, :, :].unsqueeze(2).to_broadcast(b4)
            bg = big[:, :, :].rearrange("p t (a b) -> p t a b", a=8)
            bg2 = big2[:, :, :].rearrange("p t (a b) -> p t a b", a=8)
            V.tensor_tensor(bg, other, mine, ALU.is_gt)
            V.tensor_tensor(bg2, other, mine, ALU.is_equal)
            V.tensor_reduce(small[:, 0:2], lg[:, :, :], AX, ALU.max)
            dve.drain()
            V.tensor_tensor(big2[:, :, :], big2[:, :, :], C("earlier").unsqueeze(1).to_broadcast([PART, TILES, 64]), ALU.mult)
            dve.drain()
            V.tensor_tensor(big[:, :, :], big[:, :, :], big2[:, :, :], ALU.add)
            dve.drain()
            V.tensor_reduce(rank[:, :, :], bg, AX, ALU.add)
            dve.drain()
            V.tensor_scalar(sel[:, :, :], rank[:, :, :], 2.0, None, ALU.is_lt).then_inc(sel_ready, 1)
            V.tensor_tensor(lg[:, :, :], lg[:, :, :], small[:, 0:2].unsqueeze(2).to_broadcast([PART, TILES, 8]),
                            ALU.subtract).then_inc(lg_ready, 1)
            dve.wait_ge(expl_ready, 1)
            V.tensor_tensor(lg[:, :, :], lg[:, :, :], sel[:, :, :], ALU.mult)
            dve.drain()
            V.tensor_reduce(small[:, 2:4], lg[:, :, :], AX, ALU.add)
            dve.drain()
            V.reciprocal(small[:, 4:6], small[:, 2:4])
            dve.drain()
            for half in range(2):
                V.tensor_tensor(gate[:, :, 8 * half:8 * half + 8], lg[:, :, :],
                                small[:, 4:6].unsqueeze(2).to_broadcast([PART, TILES, 8]), ALU.mult)
            dve.wait_ge(cnt_ps, 1)
            V.tensor_scalar(rank[:, :, :], ps[:, 1, 0:16].rearrange("p (t e) -> p t e", t=TILES), 1.0, None, ALU.add)
            V.tensor_scalar(over[:, :], ps[:, 1, 16:24], float(PART), None, ALU.is_gt)
            dve.drain()
            V.tensor_tensor(rank[:, :, :], rank[:, :, :], sel[:, :, :], ALU.mult)
            dve.drain()
            V.tensor_scalar(slot[:, :, 0:8], rank[:, :, :], -1.0, None, ALU.add)
            V.tensor_scalar(slot[:, :, 8:16], rank[:, :, :], -1.0 - PART, None, ALU.add)
            V.memset(overc[:, :], 0.0)
            V.memset(jobs_f[:, :], 0.0)
            dve.drain()
            for e in range(EXPERTS):
                V.tensor_tensor(overc[:, e + 1:e + 2], overc[:, e:e + 1], over[:, e:e + 1], ALU.add)
                dve.drain()
            for e in range(EXPERTS):
                V.tensor_scalar(big[:, 0, 0:8], C("iota")[:, 0:8], overc[:, e:e + 1], over[:, e:e + 1],
                                ALU.is_equal, ALU.mult)
                dve.drain()
                V.scalar_tensor_tensor(out=jobs_f[:, 8:16], in0=big[:, 0, 0:8], scalar=float(e), in1=jobs_f[:, 8:16],
                                       op0=ALU.mult, op1=ALU.add)
                dve.drain()
            V.tensor_copy(jobs_f[:, 0:8], C("iota")[:, 0:8])
            V.tensor_scalar(jobs_f[:, 16:17], overc[:, 8:9], float(EXPERTS), None, ALU.add)
            dve.drain()
            V.tensor_copy(jobs[:, :], jobs_f[0:1, :]).then_inc(jobs_ready, 1)
            dve.wait_ge(jobs_ready, 1)
            n_jobs = dve.value_load(jobs[0:1, 2 * EXPERTS:2 * EXPERTS + 1], min_val=EXPERTS, max_val=2 * EXPERTS)

            def pick_rows(job, col):
                for t in range(TILES):
                    V.tensor_scalar(pick[:, t, :], C("iota"), slot[:, t, bass.ds(col, 1)], None, ALU.is_equal)
                dve.drain()
                for t in range(TILES):
                    last = V.tensor_scalar(pickg[:, t, :], pick[:, t, :], gate[:, t, bass.ds(col, 1)], None, ALU.mult)
                last.then_inc(pick_ready, 1)

            def gathered(job):
                dve.wait_ge(xg_ps, job + 1)
                V.tensor_tensor(xT[:, :, 0:PART], tp[:, 0:2, :].rearrange("p b (c n) -> p (b c) n", c=4),
                                g_ffn.unsqueeze(2).to_broadcast([PART, KT, PART]), ALU.mult).then_inc(xg_f, 1)
                dve.wait_ge(xg_hi, job + 1)
                V.tensor_tensor(xlo[:, :, 0:PART], xT[:, :, 0:PART], xhi[:, :, 0:PART], ALU.subtract).then_inc(xg_lo, 1)

            pick_rows(0, 0)
            gathered(0)
            with dve.Fori(0, n_jobs) as j:
                e = dve.value_load(jobs[0:1, bass.ds(j + 1, 1)], min_val=0, max_val=2 * EXPERTS)
                col = dve.snap((e + 8 * (j + 1 >= EXPERTS)) % (2 * EXPERTS), min_val=0, max_val=2 * EXPERTS - 1)

                def between(i):
                    if i == BACK_AT + 1:
                        dve.wait_ge(back_ps, j + 1)
                        pick_rows(j + 1, col)
                    if i == GATHER_AT:
                        gathered(j + 1)

                swiglu(MOE, len(MOE_UP), AT_MOE, 1, sg2, actv2, ahi2, alo2, 7, 23 + 8 * j, 6 + 7 * j, len(MOE), j,
                       ahead=True, between=between)
                dve.wait_ge(scat_ps, j + 1)
                V.tensor_tensor(x[:, :, :], x[:, :, :], tp.rearrange("p (t n) c -> p t (n c)", t=TILES),
                                ALU.add).then_inc(scat_used, 1)
                dve.drain()
            norm_rows(dve, x, D, xs)
            dve.drain()
            dve.wait_ge(small_landed, small_at(DEPTH, 4))
            V.tensor_tensor(y[:, :, :], xs[:, :, :], fin_g[:, :].unsqueeze(1).to_broadcast([PART, TILES, D]),
                            ALU.mult).then_inc(y_ready, 1)

        mm = nc.tensor.matmul

        def pe_chunk(pe, chunk, c0, i, banks, lhs, tiles, first, last, per=0, l=0):
            _, _, n, k0, k = chunk
            pe.wait_ge(lo_ready, number(c0, i + 1, per, l))
            for t in range(tiles):
                for c in range(k):
                    hi, lo = lhs(k0 + c, t)
                    out = banks[:, t, 0:n]
                    mm(out, lo, whi[i % SPLIT][:, c, 0:n], start=first and c == 0, stop=False)
                    mm(out, hi, wlo[i % SPLIT][:, c, 0:n], start=False, stop=False)
                    op = mm(out, hi, whi[i % SPLIT][:, c, 0:n], start=False, stop=last and c == k - 1)
            op.then_inc(split_used, 1)
            return op

        def x_lhs(k, t):
            return xhi[:, k, t * PART:(t + 1) * PART], xlo[:, k, t * PART:(t + 1) * PART]

        def pe_linear(pe, chunks, i0, i1, c0, free, per=0, l=0):
            for i in range(i0, i1):
                g = i // 2
                if i % 2 == 0:
                    v = free(g)
                    if v is not None:
                        pe.wait_ge(acc_free[g % 2], v)
                pe_chunk(pe, chunks[i], c0, i, acc[:, g % 2], x_lhs, TILES, i % 2 == 0, i % 2 == 1, per, l)

        def pe_T(pe, nT):
            pe.wait_ge(xs_ready, nT + 1)
            for c in range(KT):
                for t in range(TILES):
                    op = nc.tensor.transpose(tp[:, c // 2, (c % 2) * S + t * PART:(c % 2) * S + (t + 1) * PART],
                                             xs[:, t, c * PART:(c + 1) * PART], ident)
                if c in (3, 7):
                    op.then_inc(xt_ps, 1)

        def pe_attention(pe, att, qk, v):
            def scores(h):
                if h >= 2:
                    pe.wait_ge(s_masked, HEADS * att + h - 1)
                q, k = qk(h)
                mm(tp[:, h % 2, 0:128], q[:, 0:128], k[:, 0:128], start=True, stop=True)
                mm(tp[:, h % 2, 128:384], q[:, 128:256], k[:, :], start=True, stop=True).then_inc(s_ps, 1)

            def weighted(h):
                pe.wait_ge(p_ready, HEADS * att + h + 1)
                if h >= 2:
                    pe.wait_ge(pT_ready, HEADS * att + h - 1)
                for b in range(3):
                    op = nc.tensor.transpose(tp[:, 2 + h % 2, 128 * b:128 * b + 128], pr[:, h % 2, 128 * b:128 * b + 128], ident)
                op.then_inc(pT_ps, 1)
                pe.wait_ge(pT_ready, HEADS * att + h + 1)
                if h >= 2:
                    pe.wait_ge(o_ready, HEADS * att + h - 1)
                o, b = 0, h % 2
                mm(ps[:, b, o:o + HD], pT[:, 0:128], v(h, 0), start=True, stop=True)
                mm(ps[:, b, o + HD:o + 2 * HD], pT[:, 128:256], v(h, 0), start=True, stop=False)
                mm(ps[:, b, o + HD:o + 2 * HD], pT[:, 256:384], v(h, 1), start=False, stop=True).then_inc(o_ps, 1)

            scores(0)
            for h in range(HEADS):
                if h + 1 < HEADS:
                    scores(h + 1)
                weighted(h)

        def tensor_program(pe):
            pe.wait_ge(const_landed, 32)
            pe.wait_ge(rows_landed, 16 * len(GAIN_ROWS))
            nc.tensor.transpose(tp[:, 0, 0:N_GAIN], g_rows, ident[0:N_GAIN, 0:N_GAIN]).then_inc(gain_ps, 1)
            pe.wait_ge(gain_ready, 1)
            n_in = len(column_chunks(D_IN))
            with pe.Fori(0, DEPTH) as l:
                pe_T(pe, 2 * l)
                pe.wait_ge(xt_lo, 4 * l + 2)

                def free(g):
                    if g < 2:
                        return (5 if g == 0 else 4) * l
                    return g // 2 + (5 if g % 2 == 0 else 4) * l
                pe_linear(pe, HYBRID, 0, n_in, AT_HYBRID, free, len(HYBRID), l)
                pe.wait_ge(cn_ready, l + 1)
                for c in range(3):
                    for t in range(TILES):
                        op = nc.tensor.transpose(tp[:, c // 2, (c % 2) * S + t * PART:(c % 2) * S + (t + 1) * PART],
                                                 P[:, t, c * PART:(c + 1) * PART], ident)
                op.then_inc(cT_ps, 1)
                pe.wait_ge(small_landed, 16 * N_SMALL * (l + 1))
                for g in range(4):
                    op = nc.tensor.transpose(tp[:, 2, g * 128:(g + 1) * 128], sgw[:, g, :], ident)
                op.then_inc(sgT_ps, 1)
                pe.wait_ge(cT_ready, l + 1)
                for t in range(TILES):
                    for c in range(2):
                        mm(acc[:, 1, t, 0:384], cT[:, c, t * PART:(t + 1) * PART], w_uq[:, c, :],
                           start=c == 0, stop=c == 1)
                    op = mm(tp[:, t, :], cT[:, 2, t * PART:(t + 1) * PART], w_ukv[:, :], start=True, stop=True)
                op.then_inc(qkv_ps, 1)
                pe.wait_ge(zv_ready, l + 1)
                z = seg("c_h")
                for j in range(2):
                    mm(ps[:, j, 0:GW], shift[:, 2 * j, :], z[:, 0, :], start=True, stop=True)
                    mm(ps[:, j, GW:2 * GW], shift[:, 2 * j, :], z[:, 1, :], start=True, stop=False)
                    op = mm(ps[:, j, GW:2 * GW], shift[:, 2 * j + 1, :], z[:, 0, :], start=False, stop=True)
                op.then_inc(conv_ps, 1)
                pe.wait_ge(sgT_ready, l + 1)
                for t in range(TILES):
                    for g in range(4):
                        a = COLS["sg_v"][0] + g * 64
                        op = mm(tp[:, 3, t * 256 + g * 64:t * 256 + g * 64 + 64], sgT[:, g, :], P[:, t, a:a + 64],
                                start=True, stop=True)
                op.then_inc(mix_ps, 1)
                pe.wait_ge(qk_ready, l + 1)
                pe.wait_ge(v_ready, l + 1)
                for src, bank in ((qn, 2), (kc, 4)):
                    for h in range(4):
                        for t in range(TILES):
                            op = nc.tensor.transpose(
                                ps[0:96, bank + h // 2, (h % 2) * S + t * PART:(h % 2) * S + (t + 1) * PART],
                                src[:, t, h, :], ident)
                    op.then_inc(qT_ps, 1)
                for name, bank in (("mq", 6), ("mk", 2)):
                    if name == "mk":
                        pe.wait_ge(qT_ready, 4 * l + 1)
                    for c in range(2):
                        for t in range(TILES):
                            a = COLS[name][0] + c * PART
                            op = nc.tensor.transpose(ps[:, bank, c * S + t * PART:c * S + (t + 1) * PART],
                                                     P[:, t, a:a + PART], ident)
                    op.then_inc(qT_ps, 1)
                pe.wait_ge(qT_ready, 4 * l + 4)

                def qk(h):
                    if h < 4:
                        return QT[0:96, h, :], KTr[0:96, h, :]
                    b = (h % 2) * HD
                    return QT[b:b + HD, 2 + h // 2, :], KTr[b:b + HD, 2 + h // 2, :]

                def v(h, t):
                    return (va if h < 4 else seg("mv"))[:, t, (h % 4) * HD:(h % 4 + 1) * HD]

                pe_attention(pe, l, qk, v)
                pe_T(pe, 2 * l + 1)
                pe.wait_ge(xt_lo, 4 * l + 4)
                pe_linear(pe, HYBRID, n_in, len(HYBRID), AT_HYBRID, free, len(HYBRID), l)

            def mixer(m, at, free0, free1):
                nT = 2 * DEPTH + 3 * m
                pe_T(pe, nT)
                pe.wait_ge(xt_lo, 2 * nT + 2)

                def free(g):
                    return (free1 if g % 2 else free0) + g // 2
                n_in = len(column_chunks(D_IN2))
                pe_linear(pe, MIXER, 0, n_in, at, free)
                pe.wait_ge(acc_free[0], free0 + 2)
                pe.wait_ge(acc_free[1], free1 + 2)
                for src, bank in ((512, 4), (1024, 6)):
                    for c in range(4):
                        for t in range(TILES):
                            op = nc.tensor.transpose(
                                ps[:, bank + c // 2, (c % 2) * S + t * PART:(c % 2) * S + (t + 1) * PART],
                                P[:, t, src + c * PART:src + (c + 1) * PART], ident)
                    op.then_inc(qT_ps, 1)
                for g in range(4):
                    o = (g % 2) * S
                    mm(ps[:, g // 2, o:o + PART], P[:, 0, g * PART:(g + 1) * PART], poolm[:, g, 0, :],
                       start=True, stop=True)
                    mm(ps[:, g // 2, o + PART:o + S], P[:, 0, g * PART:(g + 1) * PART], poolm[:, g, 1, :],
                       start=True, stop=False)
                    op = mm(ps[:, g // 2, o + PART:o + S], P[:, 1, g * PART:(g + 1) * PART], poolm[:, g, 2, :],
                            start=False, stop=True)
                op.then_inc(dT_ps, 1)
                pe.wait_ge(dT_ready, m + 1)
                pe.wait_ge(small_landed, small_at(DEPTH, m + 1))
                dT = T[:, :].rearrange("p (g t) -> p g t", g=4)
                for t in range(TILES):
                    for g in range(4):
                        op = mm(ps[:, 2 + t, g * PART:(g + 1) * PART], dT[:, g, t * PART:(t + 1) * PART], sgw[:, g, :],
                                start=True, stop=True)
                op.then_inc(z_ps, 1)
                pe.wait_ge(qT_ready, 4 * DEPTH + 2 * m + 2)

                def qk(h):
                    b = (h % 2) * HD
                    return QT[b:b + HD, h // 2, :], KTr[b:b + HD, h // 2, :]

                pe_attention(pe, DEPTH + m, qk, lambda h, t: P[:, t, 1536 + h * HD:1536 + (h + 1) * HD])
                pe_T(pe, nT + 1)
                pe.wait_ge(xt_lo, 2 * nT + 4)
                pe_linear(pe, MIXER, n_in, len(MIXER), at, free)

            def swiglu(chunks, n_up, at, tiles, actb, hib, lob, ups, free0, free1, jobsn, per=0, l=0, between=None,
                   before_T=None):
                w = tiles * PART

                def a_lhs(k, t):
                    a = k * w + t * PART
                    return hib[:, a:a + PART], lob[:, a:a + PART]

                last_k = (len(chunks) - n_up) // 2 - 1
                for i in range(len(chunks)):
                    if i < n_up:
                        g = i // 2 % 2
                        if i % 4 == 0:
                            pe.wait_ge(acc_free[0], free0 + i // 4)
                        elif i == 2:
                            pe.wait_ge(acc_free[1], free1)
                        elif i % 4 == 2:
                            pe.wait_ge(act_ready, jobsn + i // 4)
                        pe_chunk(pe, chunks[i], at, i, acc[:, g], x_lhs, tiles, i % 2 == 0, i % 2 == 1, per, l)
                    else:
                        kq, n = (i - n_up) // 2, (i - n_up) % 2
                        if kq == 0 and n == 0:
                            pe.wait_ge(acc_free[0], free0 + n_up // 4)
                        elif kq == 0:
                            pe.wait_ge(act_ready, jobsn + n_up // 4)
                        if n == 0:
                            pe.wait_ge(aT_ready, jobsn + kq + 1)
                        pe_chunk(pe, chunks[i], at, i, acc[:, n], a_lhs, tiles, kq == 0, kq == last_k, per, l)
                    if i >= 6 and (i - 6) % 4 == 0 and (i - 6) // 4 < ups:
                        j = (i - 6) // 4
                        pe.wait_ge(act_ready, jobsn + j + 1)
                        if j >= 2:
                            pe.wait_ge(aT_ready, jobsn + j - 1)
                        elif before_T:
                            before_T()
                        flat = tp[:, 2 * (j % 2):2 * (j % 2) + tiles, :].rearrange("p b n -> p (b n)")
                        for b in range(chunks[4 * j][2] // PART):
                            for t in range(tiles):
                                a = b * w + t * PART
                                op = nc.tensor.transpose(flat[:, a:a + PART], actb[:, t, b * PART:(b + 1) * PART], ident)
                        op.then_inc(aT_ps, 1)
                    if between:
                        between(i)

            mixer(0, AT_MIX0, 10, 8)
            pe_T(pe, 2 * DEPTH + 2)
            pe.wait_ge(xt_lo, 2 * (2 * DEPTH + 2) + 2)
            swiglu(FFN, len(FFN_UP), AT_FFN, TILES, actv, ahi, alo, 6, 13, 11, 0)
            mixer(1, AT_MIX1, 20, 12)
            pe_T(pe, 2 * DEPTH + 5)
            pe.wait_ge(small_landed, small_at(DEPTH, 4))
            pe.wait_ge(xt_f, 2 * (DEPTH + 2 * DEPTH + 5 - 2 * DEPTH) + 2)
            for t in range(TILES):
                for c in range(KT):
                    op = mm(ps[:, 0, t * 8:(t + 1) * 8], xT[:, c, t * PART:(t + 1) * PART], w_rt[:, c, :],
                            start=c == 0, stop=c == KT - 1)
            op.then_inc(lg_ps, 1)
            pe.wait_ge(sel_ready, 1)
            mm(ps[:, 1, 0:8], C("before"), sel[:, 0, :], start=True, stop=True)
            mm(ps[:, 1, 8:16], C("ones"), sel[:, 0, :], start=True, stop=False)
            mm(ps[:, 1, 8:16], C("before"), sel[:, 1, :], start=False, stop=True)
            mm(ps[:, 1, 16:24], C("ones"), sel[:, 0, :], start=True, stop=False)
            mm(ps[:, 1, 16:24], C("ones"), sel[:, 1, :], start=False, stop=True).then_inc(cnt_ps, 1)
            pe.wait_ge(jobs_ready, 1)
            n_jobs = pe.value_load(jobs[0:1, 2 * EXPERTS:2 * EXPERTS + 1], min_val=EXPERTS, max_val=2 * EXPERTS)

            def gather(job):
                pe.wait_ge(pick_ready, job + 1)
                for c in range(KT):
                    for t in range(TILES):
                        op = mm(tp[:, c // 4, (c % 4) * PART:(c % 4 + 1) * PART], xs[:, t, c * PART:(c + 1) * PART],
                                pick[:, t, :], start=t == 0, stop=t == TILES - 1)
                op.then_inc(xg_ps, 1)

            gather(0)
            with pe.Fori(0, n_jobs) as j:
                pe.wait_ge(xg_lo, j + 1)

                def between(i):
                    if i == BACK_AT:
                        pe.wait_ge(aT_ready, 6 + 7 * j + 7)
                        for t in range(TILES):
                            op = nc.tensor.transpose(tp[:, 2, t * PART:(t + 1) * PART], pickg[:, t, :], ident)
                        op.then_inc(back_ps, 1)
                    if i == GATHER_AT - 2:
                        gather(j + 1)

                swiglu(MOE, len(MOE_UP), AT_MOE, 1, actv2, ahi2, alo2, 7, 23 + 8 * j, 15 + j, 6 + 7 * j,
                       len(MOE), j, between=between, before_T=lambda: pe.wait_ge(scat_used, j))
                pe.wait_ge(back_ready, j + 1)
                pe.wait_ge(acc_free[1], 15 + j + 1)
                for t in range(TILES):
                    for n in range(2):
                        op = mm(tp[:, 2 * t + n, :], backT[:, t, :], yg[:, n * NC:(n + 1) * NC], start=True, stop=True)
                op.then_inc(scat_ps, 1)

        with nc.Block() as block:
            @block.sync
            def _(sp):
                sync_program(sp)

            @block.gpsimd
            def _(pool):
                pool.dma_start(x[:, :, :], A["x"].rearrange("b (t p) d -> p (b t) d", p=PART)).then_inc(x_landed, 16)
                pool_program(pool)

            @block.scalar
            def _(act):
                scalar_program(act)

            @block.vector
            def _(dve):
                dve.wait_ge(const_landed, 32)
                vector_program(dve)

            @block.tensor
            def _(pe):
                tensor_program(pe)


_INS = ["x", "positions", "norm_g", "w_in", "mla_q_norm_g", "mla_w_uq", "mla_kv_norm_g", "mla_w_ukv", "mla_q_g",
        "mla_k_nope_g", "mla_k_rope_g", "conv_w", "sg_ln_g", "sg_ln_b", "sg_w", "sg_b", "moba_q_g", "moba_k_g",
        "w_out", "norm_mix_2", "w_in_2", "w_pool_2", "pool_scale_2", "attn_gain_2", "w_out_2", "norm_ffn_2",
        "ffn_wg_2", "ffn_wu_2", "ffn_wd_2", "w_router_2", "moe_wg_2", "moe_wu_2", "moe_wd_2", "final_norm_2"]


def kernel(**inputs):
    import concourse.bacc as bacc
    from concourse.bass_utils import run_bass_kernel_spmd

    nc = bacc.Bacc("TRN2", target_bir_lowering=False, num_devices=1)
    arrays, aps = {}, {}
    for name in _INS:
        a = np.ascontiguousarray(inputs[name])
        arrays[name] = a
        aps[name] = nc.dram_tensor(name, a.shape, mybir.dt.from_np(a.dtype), kind="ExternalInput").ap()
    arrays["consts"] = shape_constants()
    aps["consts"] = nc.dram_tensor("consts", arrays["consts"].shape, F32, kind="ExternalInput").ap()
    aps["out"] = nc.dram_tensor("out", (1, S, D), F32, kind="ExternalOutput").ap()
    build(nc, aps)
    r = run_bass_kernel_spmd(nc, [arrays], core_ids=[0])
    return r.results[0]["out"]
```

```python
from contextlib import ExitStack

import numpy as np

import concourse.bass as bass
from concourse import mybir
from concourse.alu_op_type import AluOpType as ALU

F32 = mybir.dt.float32
F32R = mybir.dt.float32r
I32 = mybir.dt.int32
ACT = mybir.ActivationFunctionType
AX = mybir.AxisListType.X

PART = 128
D = 1024
S = 256
TILES = S // PART
KT = D // PART
EPS = 1e-6
NEG = -1e30
DEPTH = 2
GW = D // 4
D_IN = 3488
D_IN2 = 2048
D_FF = 2816
D_FFE = 3584
EXPERTS = 8
HEADS = 8
MLA_HEADS, MLA_QK, MLA_NOPE, MLA_ROPE = 4, 96, 64, 32
HD = 64

COLS = {}
_at = 0
for _name, _n in (("cq", 256), ("ckv", 128), ("kr", 32), ("g_a", GW), ("c_h", GW), ("c_b", GW), ("c_c", GW),
                  ("g_b", GW), ("sg_u", GW), ("sg_v", GW), ("g_c", GW), ("mq", GW), ("mk", GW), ("mv", GW),
                  ("g_d", GW)):
    COLS[_name] = (_at, _at + _n)
    _at += _n

GAIN_ROWS = (("norm_g", 2, 8), ("mla_q_norm_g", 2, 2), ("mla_kv_norm_g", 2, 1), ("sg_b", 2, 4),
             ("norm_mix_2", 2, 8), ("pool_scale_2", 2, 4), ("attn_gain_2", 2, 4), ("norm_ffn_2", 2, 8))
GAIN_AT = {}
_at = 0
for _name, _l, _n in GAIN_ROWS:
    GAIN_AT[_name] = (_at, _n)
    _at += _l * _n
N_GAIN = _at

BCAST = {}
_at = 0
for _name, _n in (("mla_q_g", 96), ("mla_k_nope_g", 64), ("mla_k_rope_g", 32), ("moba_q_g", 64),
                  ("moba_k_g", 64), ("sg_ln_g", 256), ("sg_ln_b", 256), ("conv_w", 768)):
    BCAST[_name] = (_at, _at + _n)
    _at += _n
N_BCAST = _at

CONST = {}
_at = 0
for _name, _n in (("ident", 128), ("causal", 384), ("dilated", 384), ("inv", 16), ("shift", 4 * 128),
                  ("pool", 4 * 3 * 128), ("before", 128), ("ones", 128), ("upto", 128), ("iota", 128),
                  ("earlier", 64)):
    CONST[_name] = (_at, _at + _n)
    _at += _n
N_CONST = _at


def shape_constants():
    c = np.zeros((PART, N_CONST), np.float32)
    p = np.arange(PART)

    def put(name, a):
        c[:, CONST[name][0]:CONST[name][1]] = np.asarray(a, np.float32).reshape(PART, -1)

    put("ident", np.eye(PART))
    q0, q1, k = p[:, None], p[:, None] + PART, np.arange(S)[None, :]
    put("causal", np.concatenate([np.where(k[:, :PART] <= q0, 0.0, NEG), np.where(k <= q1, 0.0, NEG)], 1))
    def count(q, k):
        d = q - k
        n = (d >= 0) * ((d <= 128) * 1 + (d % 4 == 0) * (d <= 512) + (d % 16 == 0) * (d <= 2048))
        return np.where(n > 0, np.log(np.maximum(n, 1)) * HD ** 0.5, NEG)
    put("dilated", np.concatenate([count(q0, k[:, :PART]), count(q1, k)], 1))
    inv = 500000.0 ** (-np.arange(16, dtype=np.float64) * 2.0 / 32)
    put("inv", np.broadcast_to(inv.astype(np.float32), (PART, 16)))
    s, t = p[:, None], p[None, :]
    put("shift", np.stack([s == t - 1, s == t - 1 + PART, s == t - 2, s == t - 2 + PART], 1))
    m = []
    for w in (2, 4, 8, 16):
        ss, tt = np.arange(S)[:, None], np.arange(S)[None, :]
        full = np.where((ss <= tt) & (ss > tt - w), 1.0 / np.minimum(tt + 1, w), 0.0) - (ss == tt)
        m += [full[:PART, :PART], full[:PART, PART:], full[PART:, PART:]]
    put("pool", np.stack(m, 1))
    put("before", s < t)
    put("ones", np.ones((PART, PART)))
    put("upto", s <= t)
    put("iota", np.broadcast_to(p[None, :], (PART, PART)))
    e = np.arange(8)
    put("earlier", np.broadcast_to((e[None, :] < e[:, None]).reshape(1, 64), (PART, 64)))
    return c


RAW = 6
SPLIT = 3
KC = 4
NC = 512


def column_chunks(width, order=None):
    blocks = order or range(-(-width // NC))
    return [(b * NC, min(NC, width - b * NC), k, KC) for b in blocks for k in range(0, KT, KC)]


def row_chunks(rows):
    return [(n, NC, k, min(KC, rows // PART - k)) for k in range(0, rows // PART, KC) for n in (0, NC)]


HYBRID_ORDER = (0, 4, 5, 6, 3, 1, 2)
MIXER_ORDER = (1, 2, 3, 0)
HYBRID = [("in",) + c for c in column_chunks(D_IN, HYBRID_ORDER)] + [("out",) + c for c in column_chunks(D)]
MIXER = [("in",) + c for c in column_chunks(D_IN2, MIXER_ORDER)] + [("out",) + c for c in column_chunks(D)]


def swiglu_chunks(width):
    cols = column_chunks(width)
    up = []
    for j in range(0, len(cols), 2):
        up += [("g",) + cols[j], ("g",) + cols[j + 1], ("u",) + cols[j], ("u",) + cols[j + 1]]
    return up, [("d",) + c for c in row_chunks(width)]


FFN_UP, FFN_DOWN = swiglu_chunks(D_FF)
MOE_UP, MOE_DOWN = swiglu_chunks(D_FFE)
FFN = FFN_UP + FFN_DOWN
MOE = MOE_UP + MOE_DOWN
AT_HYBRID = 0
AT_MIX0 = AT_HYBRID + DEPTH * len(HYBRID)
AT_FFN = AT_MIX0 + len(MIXER)
AT_MIX1 = AT_FFN + len(FFN)
AT_MOE = AT_MIX1 + len(MIXER)
BACK_AT = len(MOE_UP) + 4
GATHER_AT = len(MOE_UP) + 9
assert all(n % RAW == 0 for n in (len(HYBRID), AT_MIX0, AT_FFN, AT_MIX1, AT_MOE, len(MOE)))


def build(nc, A):
    ctx = ExitStack()
    with ctx:
        def sb(name, shape, dt=F32, stack=ctx):
            name = f"{name}_sb"
            return stack.enter_context(nc.sbuf_tensor(name, shape, dt))

        def sem(name):
            return ctx.enter_context(nc.semaphore(name))

        raw = [sb(f"raw{i}", [PART, KC, NC]) for i in range(RAW)]
        whi = [sb(f"whi{i}", [PART, KC, NC], F32R) for i in range(SPLIT)]
        wlo = [sb(f"wlo{i}", [PART, KC, NC], F32R) for i in range(SPLIT)]
        x = sb("x", [PART, TILES, D])
        xs = sb("xs", [PART, TILES, D])
        xT = sb("xT", [PART, KT, S])
        xhi = sb("xhi", [PART, KT, S], F32R)
        xlo = sb("xlo", [PART, KT, S], F32R)
        con = sb("con", [PART, N_CONST])
        gain = sb("gain", [PART, N_GAIN])
        pos = sb("pos", [PART, TILES], I32)
        trig = sb("trig", [PART, 2, TILES, 16])
        stat = sb("stat", [PART, 40])
        rs = sb("rs", [PART, 40])
        rs_tmp = sb("rs_tmp", [PART, 16])
        negm = sb("negm", [PART, HEADS, TILES])
        den = sb("den", [PART, HEADS, TILES])
        rden = sb("rden", [PART, HEADS, TILES])

        mixed = ExitStack()
        P = sb("P", [PART, TILES, D_IN], stack=mixed)
        QT = sb("QT", [PART, 6, S], stack=mixed)
        KTr = sb("KTr", [PART, 6, S], stack=mixed)
        T = sb("T", [PART, 1024], stack=mixed)
        w_uq = sb("w_uq", [PART, 2, 384], stack=mixed)
        w_ukv = sb("w_ukv", [PART, 512], stack=mixed)
        sgw = sb("sgw", [PART, 4, 128], stack=mixed)
        bc = sb("bc", [PART, N_BCAST], stack=mixed)
        mixed.close()
        swi = ExitStack()
        sg = sb("sg", [PART, TILES, NC], stack=swi)
        actv = sb("actv", [PART, TILES, NC], stack=swi)
        ahi = sb("ahi", [PART, D_FF // PART * S], F32R, stack=swi)
        alo = sb("alo", [PART, D_FF // PART * S], F32R, stack=swi)
        swi.close()
        moe = ExitStack()
        sg2 = sb("sg2", [PART, 1, NC], stack=moe)
        actv2 = sb("actv2", [PART, 1, NC], stack=moe)
        ahi2 = sb("ahi2", [PART, D_FFE], F32R, stack=moe)
        alo2 = sb("alo2", [PART, D_FFE], F32R, stack=moe)
        yg = sb("yg", [PART, D], stack=moe)
        pick = sb("pick", [PART, TILES, PART], stack=moe)
        pickg = sb("pickg", [PART, TILES, PART], stack=moe)
        backT = sb("backT", [PART, TILES, PART], stack=moe)
        w_rt = sb("w_rt", [PART, KT, EXPERTS], stack=moe)
        lg = sb("lg", [PART, TILES, EXPERTS], stack=moe)
        big = sb("big", [PART, TILES, 64], stack=moe)
        big2 = sb("big2", [PART, TILES, 64], stack=moe)
        rank = sb("rank", [PART, TILES, EXPERTS], stack=moe)
        sel = sb("sel", [PART, TILES, EXPERTS], stack=moe)
        gate = sb("gate", [PART, TILES, 2 * EXPERTS], stack=moe)
        slot = sb("slot", [PART, TILES, 2 * EXPERTS], stack=moe)
        small = sb("small", [PART, 8], stack=moe)
        over = sb("over", [PART, EXPERTS], stack=moe)
        overc = sb("overc", [PART, EXPERTS + 2], stack=moe)
        jobs_f = sb("jobs_f", [PART, 2 * EXPERTS + 1], stack=moe)
        jobs = sb("jobs", [1, 2 * EXPERTS + 1], I32, stack=moe)
        fin_g = sb("fin_g", [PART, D], stack=moe)
        moe.close()
        g_rows = raw[RAW - 1][0:N_GAIN, 0, 0:PART]

        ps = ctx.enter_context(nc.psum_tensor("ps", [PART, 8, NC], F32))
        acc = ps[:, 0:4, :].rearrange("p (a t) n -> p a t n", a=2)
        tp = ps[:, 4:8, :]

        raw_landed = [sem(f"raw_landed{i}") for i in range(RAW)]
        hi_ready = sem("hi_ready")
        lo_ready = sem("lo_ready")
        split_used = sem("split_used")
        acc_free = [sem(f"acc_free{i}") for i in range(2)]
        const_landed = sem("const_landed")
        rows_landed = sem("rows_landed")
        pos_landed = sem("pos_landed")
        x_landed = sem("x_landed")
        small_landed = sem("small_landed")
        gain_ps = sem("gain_ps")
        gain_ready = sem("gain_ready")
        angle_ready = sem("angle_ready")
        trig_ready = sem("trig_ready")
        xs_ready = sem("xs_ready")
        xt_ps = sem("xt_ps")
        xt_f = sem("xt_f")
        xt_hi = sem("xt_hi")
        xt_lo = sem("xt_lo")
        gates_ready = sem("gates_ready")
        cn_ready = sem("cn_ready")
        cT_ps = sem("cT_ps")
        cT_ready = sem("cT_ready")
        sgT_ps = sem("sgT_ps")
        sgT_ready = sem("sgT_ready")
        z_ready = sem("z_ready")
        vn_ready = sem("vn_ready")
        mqk_ready = sem("mqk_ready")
        qkv_ps = sem("qkv_ps")
        conv_ps = sem("conv_ps")
        mix_ps = sem("mix_ps")
        sq_ready = sem("sq_ready")
        v_ready = sem("v_ready")
        qk_ready = sem("qk_ready")
        qT_ps = sem("qT_ps")
        qT_ready = sem("qT_ready")
        s_ps = sem("s_ps")
        s_masked = sem("s_masked")
        p_ready = sem("p_ready")
        pT_ps = sem("pT_ps")
        pT_ready = sem("pT_ready")
        o_ps = sem("o_ps")
        o_ready = sem("o_ready")
        layer_done = sem("layer_done")
        dT_ps = sem("dT_ps")
        dT_ready = sem("dT_ready")
        z_ps = sem("z_ps")
        act_ready = sem("act_ready")
        aT_ps = sem("aT_ps")
        ahi_ready = sem("ahi_ready")
        aT_ready = sem("aT_ready")
        lg_ps = sem("lg_ps")
        expl_ready = sem("expl_ready")
        lg_ready = sem("lg_ready")
        sel_ready = sem("sel_ready")
        cnt_ps = sem("cnt_ps")
        jobs_ready = sem("jobs_ready")
        pick_ready = sem("pick_ready")
        back_ps = sem("back_ps")
        xg_ps = sem("xg_ps")
        xg_f = sem("xg_f")
        xg_hi = sem("xg_hi")
        xg_lo = sem("xg_lo")
        back_ready = sem("back_ready")
        scat_ps = sem("scat_ps")
        scat_used = sem("scat_used")
        y_ready = sem("y_ready")
        out_written = sem("out_written")

        def C(name):
            a, b = CONST[name]
            return con[:, a:b]

        ident = C("ident")
        shift = C("shift").rearrange("p (j t) -> p j t", j=4)
        poolm = C("pool").rearrange("p (g j t) -> p g j t", g=4, j=3)

        def G(name, l):
            a, n = GAIN_AT[name]
            return gain[:, a + l * n:a + (l + 1) * n]

        def Gl(name, l):
            a, n = GAIN_AT[name]
            return gain[:, bass.ds(a + l * n, n)]

        def B(name):
            a, b = BCAST[name]
            return bc[:, a:b]

        def seg(name):
            a, b = COLS[name]
            return P[:, :, a:b]

        y = xs
        xT_flat = xT[:, :, :].rearrange("p a b -> p (a b)")
        qn = xT_flat[:, 0:768].rearrange("p (t h n) -> p t h n", t=TILES, h=MLA_HEADS)
        sgT = y[:, :, 512:768].rearrange("p t (g n) -> p t g n", g=2)
        sm = xT_flat[:, 0:768].rearrange("p (r n) -> p r n", r=2)
        pr = xT_flat[:, 768:1536].rearrange("p (r n) -> p r n", r=2)
        pT = xT_flat[:, 1536:1920]
        rt = T[:, 0:4 * 128].rearrange("p (j n) -> p j n", j=4)
        cT = T[:, 0:768].rearrange("p (c n) -> p c n", c=3)
        kc = P[:, :, 0:384].rearrange("p t (h n) -> p t h n", h=MLA_HEADS)
        va = T[:, 512:1024].rearrange("p (t n) -> p t n", t=TILES)

        def number(c0, i, per=0, l=0):
            return c0 + i + per * l

        def landed(c0, i, per=0, l=0):
            return 16 * (c0 // RAW + i // RAW + 1) + 16 * (per // RAW) * l

        def sp_chunk(sp, src, c0, i, shape, per=0, l=0):
            n0, n, k0, k = shape
            if c0 + i >= RAW:
                sp.wait_ge(lo_ready, number(c0, i - RAW + 1, per, l))
            sp.dma_start(raw[i % RAW][:, 0:k, 0:n],
                         src(k0 * PART, k * PART, n0, n)).then_inc(raw_landed[i % RAW], 16)

        def rows(w, l):
            def cut(r0, r, n0, n):
                if isinstance(l, int):
                    return w[l, r0:r0 + r, n0:n0 + n].rearrange("(c p) n -> p c n", p=PART)
                return w[bass.ds(l, 1), r0:r0 + r, n0:n0 + n].rearrange("a (c p) n -> p (a c) n", p=PART)
            return cut

        def sp_part(sp, chunks, srcs, c0, per=0, l=0):
            for i, (which, *shape) in enumerate(chunks):
                sp_chunk(sp, srcs[which], c0, i, shape, per, l)

        def sync_program(sp):
            hybrid0 = {"in": rows(A["w_in"], 0), "out": rows(A["w_out"], 0)}
            for i, (which, *shape) in enumerate(HYBRID):
                if i == RAW - 1:
                    sp.wait_ge(gain_ps, 1)
                sp_chunk(sp, hybrid0[which], AT_HYBRID, i, shape)
            with sp.Fori(1, DEPTH) as l:
                sp_part(sp, HYBRID, {"in": rows(A["w_in"], l), "out": rows(A["w_out"], l)},
                        AT_HYBRID + len(HYBRID), len(HYBRID), l - 1)
            for m, at in ((0, AT_MIX0), (1, AT_MIX1)):
                sp_part(sp, MIXER, {"in": rows(A["w_in_2"], m), "out": rows(A["w_out_2"], m)}, at)
                if m == 0:
                    sp_part(sp, FFN, {"g": rows(A["ffn_wg_2"], 0), "u": rows(A["ffn_wu_2"], 0),
                                      "d": rows(A["ffn_wd_2"], 0)}, AT_FFN)

            def expert(j, e):
                sp_part(sp, MOE, {"g": rows(wg, e), "u": rows(wu, e), "d": rows(wd, e)},
                        AT_MOE, len(MOE), j)

            wg, wu, wd = (A[n].rearrange("a e k n -> (a e) k n") for n in ("moe_wg_2", "moe_wu_2", "moe_wd_2"))
            with sp.Fori(0, EXPERTS) as j:
                expert(j, j)
            sp.wait_ge(jobs_ready, 1)
            n_jobs = sp.value_load(jobs[0:1, 2 * EXPERTS:2 * EXPERTS + 1], min_val=EXPERTS, max_val=2 * EXPERTS)
            with sp.If(n_jobs > EXPERTS):
                with sp.Fori(EXPERTS, n_jobs) as j:
                    e = sp.value_load(jobs[0:1, bass.ds(j, 1)], min_val=0, max_val=EXPERTS - 1)
                    expert(j, e)
            with sp.Else():
                sp.nop()
            for i in range(SPLIT):
                _, *shape = MOE[i]
                sp_chunk(sp, rows(wg, 0), AT_MOE, i, shape, len(MOE), n_jobs)
            sp.wait_ge(y_ready, 1)
            sp.dma_start(A["out"].rearrange("b (t p) d -> p (b t) d", p=PART), y[:, :, :]).then_inc(out_written, 16)
            sp.wait_ge(out_written, 16)

        N_SMALL = 11

        def pool_program(pool):
            with pool.Fori(0, DEPTH) as l:
                pool.wait_ge(layer_done, l + 1)
                pool.dma_start(w_uq[:, :, :], A["mla_w_uq"][bass.ds(l, 1), :, :].rearrange(
                    "a (c p) n -> p (a c) n", p=PART)).then_inc(small_landed, 16)
                pool.dma_start(w_ukv[:, :], A["mla_w_ukv"][bass.ds(l, 1), :, :].rearrange(
                    "a p n -> p (a n)")).then_inc(small_landed, 16)
                pool.dma_start(sgw[:, :, :], A["sg_w"][bass.ds(l, 1), :, :, :].rearrange(
                    "a g t s -> t (a g) s")).then_inc(small_landed, 16)
                for name, (a, b) in BCAST.items():
                    src = A[name]
                    if name == "conv_w":
                        src = src.rearrange("l w c -> l (w c)")
                    src = src[bass.ds(l, 1), :]
                    pool.dma_start(bc[:, a:b], src.to_broadcast([PART, b - a])).then_inc(small_landed, 16)
            for m in range(2):
                pool.wait_ge(layer_done, 1 + DEPTH + 2 * m)
                pool.dma_start(sgw[:, :, :], A["w_pool_2"][m].rearrange("g c e -> c g e")).then_inc(small_landed, 16)
            pool.wait_ge(layer_done, 1 + DEPTH + 3)
            pool.dma_start(w_rt[:, :, :], A["w_router_2"].rearrange("a (c p) e -> p (a c) e", p=PART)).then_inc(small_landed, 16)
            pool.dma_start(fin_g[:, :], A["final_norm_2"].rearrange("(a d) -> a d", a=1).to_broadcast(
                [PART, D])).then_inc(small_landed, 16)

        def small_at(layers, extra=0):
            return 16 * N_SMALL * layers + 16 * extra

        def act_hi(act, chunks, c0, i, per=0, l=0):
            _, _, n, _, k = chunks[i % len(chunks)]
            act.wait_ge(raw_landed[i % RAW], landed(c0, i, per, l))
            if not (isinstance(l, int) and c0 + i + per * l < SPLIT):
                act.wait_ge(split_used, number(c0, i - SPLIT + 1, per, l))
            for c in range(0, k, k // 2):
                nc.scalar.activation(whi[i % SPLIT][:, c:c + k // 2, 0:n], raw[i % RAW][:, c:c + k // 2, 0:n],
                                     ACT.Copy).then_inc(hi_ready, 1)

        def act_hiT(act, nT, with_gain):
            for h in range(2):
                if with_gain:
                    act.wait_ge(xt_f, 2 * nT[0] + h + 1)
                    src = xT[:, 4 * h:4 * h + 4, :]
                else:
                    act.wait_ge(xt_ps, 2 * nT[1] + h + 1)
                    src = tp[:, 2 * h:2 * h + 2, :].rearrange("p b (c n) -> p (b c) n", c=2)
                nc.scalar.activation(xhi[:, 4 * h:4 * h + 4, :], src, ACT.Copy).then_inc(xt_hi, 1)

        def act_exps(act, att, h, scales):
            act.wait_ge(s_masked, HEADS * att + h + 1)
            if h >= 2:
                act.wait_ge(pT_ps, HEADS * att + h - 1)
            r = h % 2
            nc.scalar.activation(pr[:, r, 0:128], sm[:, r, 0:128], ACT.Exp, bias=negm[:, h, 0:1],
                                 scale=scales[h], accum_out=den[:, h, 0:1])
            nc.scalar.activation(pr[:, r, 128:384], sm[:, r, 128:384], ACT.Exp, bias=negm[:, h, 1:2],
                                 scale=scales[h], accum_out=den[:, h, 1:2]).then_inc(p_ready, 1)

        def act_heads(act, att, heads, scales):
            for h in heads:
                act.wait_ge(pT_ps, HEADS * att + h + 1)
                if h >= 1:
                    act.wait_ge(o_ps, HEADS * att + h)
                nc.scalar.activation(pT, tp[:, 2, 0:384], ACT.Copy).then_inc(pT_ready, 1)
                if h + 2 < HEADS:
                    act_exps(act, att, h + 2, scales)

        def copy_proj(act, g, width, used):
            n0 = (HYBRID_ORDER if width == D_IN else MIXER_ORDER)[g] * NC
            n = min(NC, width - n0)
            act.wait_ge(split_used, used)
            nc.scalar.activation(P[:, :, n0:n0 + n], acc[:, g % 2, :, 0:n], ACT.Copy).then_inc(acc_free[g % 2], 1)

        def scalar_program(act):
            act.dma_start(pos[:, :], A["positions"].rearrange("b (t p) -> p (b t)", p=PART),
                          allow_slow_non_contiguous=True).then_inc(pos_landed, 16)
            act.dma_start(con[:, :], A["consts"]).then_inc(const_landed, 16)
            act.dma_start(x[:, :, :], A["x"].rearrange("b (t p) d -> p (b t) d", p=PART)).then_inc(x_landed, 16)
            for name, n_l, n in GAIN_ROWS:
                a = GAIN_AT[name][0]
                src = A[name]
                if name == "sg_b":
                    src = src.rearrange("l g t -> (l g) t")
                else:
                    src = src.rearrange("l (c p) -> (l c) p", p=PART)
                act.dma_start(raw[RAW - 1][a:a + n_l * n, 0, 0:PART], src).then_inc(rows_landed, 16)
            act.wait_ge(angle_ready, 1)
            nc.scalar.activation(trig[:, :, :, :], T[:, 0:64].rearrange("p (a t n) -> p a t n", a=2, t=TILES),
                                 ACT.Sin).then_inc(trig_ready, 1)
            for i in range(SPLIT):
                act_hi(act, HYBRID, AT_HYBRID, i)
            n_in = len(column_chunks(D_IN))
            with act.Fori(0, DEPTH) as l:
                act_hiT(act, (l, None), True)
                scales = [MLA_QK ** -0.5] * 4 + [HD ** -0.5] * 4
                for i in range(n_in):
                    if i >= 10:
                        act_heads(act, l, (2 * i - 20, 2 * i - 19), scales)
                    act_hi(act, HYBRID, AT_HYBRID, i + SPLIT, len(HYBRID), l)
                    if i % 2:
                        copy_proj(act, i // 2, D_IN, number(AT_HYBRID, i + 1, len(HYBRID), l))
                    if i == 4:
                        act.wait_ge(qkv_ps, l + 1)
                        nc.scalar.activation(xs[:, :, 0:384], tp[:, 2:4, 0:384], ACT.Square)
                        kv_ps = tp[:, 0:2, :].rearrange("p t (h n) -> p t h n", h=MLA_HEADS)
                        for t in range(TILES):
                            last = nc.scalar.activation(xs[:, t, 384:640].rearrange("p (h n) -> p h n", h=MLA_HEADS),
                                                        kv_ps[:, t, :, 0:64], ACT.Square)
                        last.then_inc(sq_ready, 1)
                        for t in range(TILES):
                            last = nc.scalar.activation(va[:, t, :].rearrange("p (h n) -> p h n", h=MLA_HEADS),
                                                        kv_ps[:, t, :, 64:128], ACT.Copy)
                        last.then_inc(v_ready, 1)
                    if i == 6:
                        act.wait_ge(qT_ps, 4 * l + 1)
                        nc.scalar.activation(QT[0:96, 0:4, :], tp[0:96, 0:2, :].rearrange("p b (c n) -> p (b c) n", c=2),
                                             ACT.Copy).then_inc(qT_ready, 1)
                        act.wait_ge(qT_ps, 4 * l + 2)
                        nc.scalar.activation(KTr[0:96, 0:4, :], tp[0:96, 2:4, :].rearrange("p b (c n) -> p (b c) n", c=2),
                                             ACT.Copy).then_inc(qT_ready, 1)
                    if i == 8:
                        act.wait_ge(qT_ps, 4 * l + 3)
                        nc.scalar.activation(QT[:, 4:6, :], tp[:, 0, :].rearrange("p (c n) -> p c n", c=2),
                                             ACT.Copy).then_inc(qT_ready, 1)
                        act.wait_ge(qT_ps, 4 * l + 4)
                        nc.scalar.activation(KTr[:, 4:6, :], tp[:, 1, :].rearrange("p (c n) -> p c n", c=2),
                                             ACT.Copy).then_inc(qT_ready, 1)
                    if i == 9:
                        act_exps(act, l, 0, scales)
                        act_exps(act, l, 1, scales)
                act.drain()
                for name in ("g_a", "g_b", "g_c", "g_d"):
                    last = nc.scalar.activation(seg(name), seg(name), ACT.Silu)
                last.then_inc(gates_ready, 1)
                act_hiT(act, (None, 2 * l + 1), False)
                for i in range(n_in, len(HYBRID)):
                    act_hi(act, HYBRID, AT_HYBRID, i + SPLIT, len(HYBRID), l)

            def mixer(m, at):
                act_hiT(act, (DEPTH + 3 * m, None), True)
                n_in = len(column_chunks(D_IN2))
                att, scales = DEPTH + m, [HD ** -0.5] * HEADS
                for i in range(n_in):
                    if i >= 6:
                        act_heads(act, att, (2 * i - 12, 2 * i - 11), scales)
                    act_hi(act, MIXER, at, i + SPLIT)
                    if i % 2:
                        copy_proj(act, i // 2, D_IN2, number(at, i + 1))
                    if i == 4:
                        q = 4 * DEPTH + 2 * m
                        act.wait_ge(qT_ps, q + 1)
                        nc.scalar.activation(QT[:, 0:4, :], tp[:, 0:2, :].rearrange("p b (c n) -> p (b c) n", c=2),
                                             ACT.Copy).then_inc(qT_ready, 1)
                        act.wait_ge(qT_ps, q + 2)
                        nc.scalar.activation(KTr[:, 0:4, :], tp[:, 2:4, :].rearrange("p b (c n) -> p (b c) n", c=2),
                                             ACT.Copy).then_inc(qT_ready, 1)
                    if i == 5:
                        act_exps(act, att, 0, scales)
                        act_exps(act, att, 1, scales)
                act.wait_ge(dT_ps, m + 1)
                nc.scalar.activation(T[:, :], ps[:, 0:2, :].rearrange("p b n -> p (b n)"), ACT.Copy).then_inc(dT_ready, 1)
                act_heads(act, att, range(4, HEADS), scales)
                act_hiT(act, (DEPTH + 3 * m + 1, None), True)
                for i in range(n_in, len(MIXER)):
                    if m == 0:
                        act_hi(act, MIXER, at, i + SPLIT)
                    elif i + SPLIT < len(MIXER):
                        act_hi(act, MIXER, at, i + SPLIT)

            def swiglu(chunks, n_up, at, tiles, sgb, hib, ups, jobsn, per=0, l=0, ahead=False, between=None):
                for i in range(len(chunks)):
                    if i + SPLIT < len(chunks) or ahead:
                        act_hi(act, chunks, at, i + SPLIT, per, l)
                    if i < n_up and i % 4 == 2:
                        j = i // 4
                        n = chunks[i][2]
                        act.wait_ge(split_used, number(at, i, per, l))
                        if not (isinstance(jobsn, int) and jobsn + j == 0):
                            act.wait_ge(act_ready, jobsn + j)
                        nc.scalar.activation(sgb[:, 0:tiles, 0:n], acc[:, 0, 0:tiles, 0:n], ACT.Silu).then_inc(acc_free[0], 1)
                    if i >= 6 and (i - 6) % 4 == 0 and (i - 6) // 4 < ups:
                        j = (i - 6) // 4
                        nb = chunks[4 * j][2] // PART
                        act.wait_ge(aT_ps, jobsn + j + 1)
                        w = tiles * PART
                        src = tp[:, 2 * (j % 2):2 * (j % 2) + tiles, :].rearrange("p b n -> p (b n)")[:, 0:nb * w]
                        nc.scalar.activation(hib[:, 4 * j * w:4 * j * w + nb * w], src, ACT.Copy).then_inc(ahi_ready, 1)
                    if between:
                        between(i)

            mixer(0, AT_MIX0)
            act_hiT(act, (DEPTH + 2, None), True)
            swiglu(FFN, len(FFN_UP), AT_FFN, TILES, sg, ahi, 6, 0, ahead=True)
            mixer(1, AT_MIX1)
            for i in range(SPLIT):
                act_hi(act, MOE, AT_MOE, i)
            act.wait_ge(lg_ready, 1)
            nc.scalar.activation(lg[:, :, :], lg[:, :, :], ACT.Exp).then_inc(expl_ready, 1)
            act.wait_ge(jobs_ready, 1)
            n_jobs = act.value_load(jobs[0:1, 2 * EXPERTS:2 * EXPERTS + 1], min_val=EXPERTS, max_val=2 * EXPERTS)

            def gathered(job):
                act.wait_ge(xg_f, job + 1)
                nc.scalar.activation(xhi[:, :, 0:PART], xT[:, :, 0:PART], ACT.Copy).then_inc(xg_hi, 1)

            gathered(0)
            with act.Fori(0, n_jobs) as j:

                def between(i):
                    if i == BACK_AT:
                        act.wait_ge(back_ps, j + 1)
                        nc.scalar.activation(backT[:, :, :], tp[:, 2, 0:256].rearrange("p (t n) -> p t n", t=TILES),
                                             ACT.Copy).then_inc(back_ready, 1)
                    if i == GATHER_AT:
                        gathered(j + 1)

                swiglu(MOE, len(MOE_UP), AT_MOE, 1, sg2, ahi2, 7, 6 + 7 * j, len(MOE), j, ahead=True, between=between)
                for n in range(2):
                    act.wait_ge(split_used, number(AT_MOE, len(MOE) - 1 + n, len(MOE), j))
                    nc.scalar.activation(yg[:, n * NC:(n + 1) * NC], acc[:, n, 0, :], ACT.Copy).then_inc(acc_free[n], 1)

        V = nc.vector

        def dve_lo(dve, chunks, c0, i, per=0, l=0):
            _, _, n, _, k = chunks[i % len(chunks)]
            for c in range(0, k, k // 2):
                dve.wait_ge(hi_ready, 2 * c0 + 2 * i + (2 if c else 1) + 2 * per * l)
                op = V.tensor_tensor(wlo[i % SPLIT][:, c:c + k // 2, 0:n], raw[i % RAW][:, c:c + k // 2, 0:n],
                                     whi[i % SPLIT][:, c:c + k // 2, 0:n], ALU.subtract)
            op.then_inc(lo_ready, 1)

        def rsqrt(dve, v, out, tmp):
            V.tensor_scalar(out.bitcast(I32), v.bitcast(I32), 1, None, ALU.logical_shift_right)
            dve.drain()
            V.tensor_scalar(out.bitcast(I32), out.bitcast(I32), -1.0, float(0x5f3759df), ALU.mult, ALU.add)
            for _ in range(3):
                dve.drain()
                V.tensor_tensor(tmp, out, out, ALU.mult)
                dve.drain()
                V.scalar_tensor_tensor(out=tmp, in0=tmp, scalar=-0.5, in1=v, op0=ALU.mult, op1=ALU.mult)
                dve.drain()
                V.scalar_tensor_tensor(out=out, in0=tmp, scalar=1.5, in1=out, op0=ALU.add, op1=ALU.mult)
            dve.drain()

        def norm_rows(dve, src, width, out, acol=0):
            for t in range(TILES):
                V.tensor_tensor_reduce(out=out[:, t, :], in0=src[:, t, :], in1=src[:, t, :], scale=1.0 / width,
                                       scalar=EPS, op0=ALU.mult, op1=ALU.add, accum_out=stat[:, t:t + 1])
            dve.drain()
            rsqrt(dve, stat[:, 0:2], rs[:, 0:2], rs_tmp[:, 0:2])
            for t in range(TILES):
                last = V.tensor_scalar(out[:, t, :], src[:, t, :], rs[:, t:t + 1], None, ALU.mult)
            return last

        def dve_T(dve, nT, nF, g):
            for h in range(2):
                dve.wait_ge(xt_ps, 2 * nT + h + 1)
                if g is not None:
                    V.tensor_tensor(xT[:, 4 * h:4 * h + 4, :],
                                    tp[:, 2 * h:2 * h + 2, :].rearrange("p b (c n) -> p (b c) n", c=2),
                                    g(h).unsqueeze(2).to_broadcast([PART, 4, S]), ALU.mult).then_inc(xt_f, 1)
            for h in range(2):
                dve.wait_ge(xt_hi, 2 * nT + h + 1)
                src = (xT[:, 4 * h:4 * h + 4, :] if g is not None else
                       tp[:, 2 * h:2 * h + 2, :].rearrange("p b (c n) -> p (b c) n", c=2))
                V.tensor_tensor(xlo[:, 4 * h:4 * h + 4, :], src, xhi[:, 4 * h:4 * h + 4, :],
                                ALU.subtract).then_inc(xt_lo, 1)

        def dve_masked(dve, att, h, mask, scales):
            r = h % 2
            dve.wait_ge(s_ps, HEADS * att + h + 1)
            if h >= 2:
                dve.wait_ge(p_ready, HEADS * att + h - 1)
            V.tensor_tensor(sm[:, r, :], tp[:, r, 0:384], mask, ALU.add)
            dve.drain()
            V.tensor_reduce(negm[:, h, 0:1], sm[:, r, 0:128], AX, ALU.max)
            V.tensor_reduce(negm[:, h, 1:2], sm[:, r, 128:384], AX, ALU.max)
            dve.drain()
            V.tensor_scalar(negm[:, h, :], negm[:, h, :], -scales[h], None, ALU.mult).then_inc(s_masked, 1)

        def dve_heads(dve, att, heads, mask, scales, at_col):
            for h in heads:
                if h + 2 < HEADS:
                    dve_masked(dve, att, h + 2, mask, scales)
                dve.wait_ge(p_ready, HEADS * att + h + 1)
                V.reciprocal(rden[:, h, :], den[:, h, :])
                dve.drain()
                dve.wait_ge(o_ps, HEADS * att + h + 1)
                src = tp[:, 3, 0:2 * HD].rearrange("p (t n) -> p t n", t=TILES)
                at = at_col(h)
                V.tensor_tensor(y[:, :, at:at + HD], src, rden[:, h, :].unsqueeze(2).to_broadcast([PART, TILES, HD]),
                                ALU.mult).then_inc(o_ready, 1)

        def rope(dve, v1, v2, o1, o2, heads, half, step):
            shp = [PART, TILES, heads, half]
            cs, sn = (trig[:, j, :, 0:16:step].unsqueeze(2).to_broadcast(shp) for j in range(2))
            n = TILES * heads * half
            t = [rt[:, j, 0:n].rearrange("p (t h n) -> p t h n", t=TILES, h=heads) for j in range(4)]
            V.tensor_tensor(t[0], v1, cs, ALU.mult)
            V.tensor_tensor(t[1], v2, sn, ALU.mult)
            V.tensor_tensor(t[2], v2, cs, ALU.mult)
            V.tensor_tensor(t[3], v1, sn, ALU.mult)
            dve.drain()
            V.tensor_tensor(o1, t[0], t[1], ALU.subtract)
            V.tensor_tensor(o2, t[2], t[3], ALU.add)
            dve.drain()

        def add_out(dve, chunks, n_in, c0, per=0, l=0, last_part=False):
            for i in range(n_in, len(chunks)):
                if not last_part or i + SPLIT < len(chunks):
                    dve_lo(dve, chunks, c0, i + SPLIT, per, l)
                if i % 2:
                    g = i // 2
                    n0 = (i - n_in) // 2 * NC
                    dve.wait_ge(split_used, number(c0, i + 1, per, l))
                    V.tensor_tensor(x[:, :, n0:n0 + NC], x[:, :, n0:n0 + NC], acc[:, g % 2, :, :],
                                    ALU.add).then_inc(acc_free[g % 2], 1)
            dve.drain()

        def latents(dve, l):
            dve.wait_ge(acc_free[0], 5 * l + 1)
            V.tensor_tensor(xs[:, :, 0:416], P[:, :, 0:416], P[:, :, 0:416], ALU.mult)
            dve.drain()
            V.tensor_reduce(stat[:, 0:2], xs[:, :, 0:256], AX, ALU.add)
            V.tensor_reduce(stat[:, 2:4], xs[:, :, 256:384], AX, ALU.add)
            V.tensor_reduce(stat[:, 4:6], xs[:, :, 384:416], AX, ALU.add)
            dve.drain()
            for a, b, n in ((0, 2, 256), (2, 4, 128), (4, 6, 32)):
                V.tensor_scalar(stat[:, a:b], stat[:, a:b], 1.0 / n, EPS, ALU.mult, ALU.add)
            dve.drain()
            rsqrt(dve, stat[:, 0:6], rs[:, 0:6], rs_tmp[:, 0:6])
            V.tensor_tensor(seg("cq"), seg("cq"), rs[:, 0:2].unsqueeze(2).to_broadcast([PART, TILES, 256]), ALU.mult)
            V.tensor_tensor(seg("ckv"), seg("ckv"), rs[:, 2:4].unsqueeze(2).to_broadcast([PART, TILES, 128]),
                            ALU.mult).then_inc(cn_ready, 1)

        def shared_k(dve, l):
            dve.wait_ge(small_landed, 16 * N_SMALL * (l + 1))
            kr = seg("kr")
            V.tensor_tensor(kr, kr, rs[:, 4:6].unsqueeze(2).to_broadcast([PART, TILES, 32]), ALU.mult)
            dve.drain()
            V.tensor_tensor(kr, kr, B("mla_k_rope_g").unsqueeze(1).to_broadcast([PART, TILES, 32]), ALU.mult)
            dve.drain()
            kr4 = kr.unsqueeze(2)
            rope(dve, kr4[:, :, :, 0:16], kr4[:, :, :, 16:32], kr4[:, :, :, 0:16], kr4[:, :, :, 16:32], 1, 16, 1)

        def latents_T(dve, l):
            dve.wait_ge(cT_ps, l + 1)
            a_q, a_kv = GAIN_AT["mla_q_norm_g"][0], GAIN_AT["mla_kv_norm_g"][0]
            V.tensor_tensor(cT[:, 0:2, :], tp[:, 0, :].rearrange("p (c n) -> p c n", c=2),
                            gain[:, bass.ds(a_q + l * 2, 2)].unsqueeze(2).to_broadcast([PART, 2, S]), ALU.mult)
            V.tensor_scalar(cT[:, 2, :], tp[:, 1, 0:S], gain[:, bass.ds(a_kv + l, 1)], None,
                            ALU.mult).then_inc(cT_ready, 1)

        mqk = P[:, :, COLS["mq"][0]:COLS["mk"][1]]
        mqk4 = mqk.rearrange("p t (h n) -> p t h n", h=8)

        def block_stats(dve, l):
            dve.wait_ge(acc_free[1], 4 * l + 1)
            dve.wait_ge(acc_free[0], 5 * l + 2)
            V.tensor_tensor(xs[:, :, 0:512], mqk, mqk, ALU.mult)
            dve.drain()
            V.tensor_reduce(stat[:, 6:22].rearrange("p (t h) -> p t h", t=TILES),
                            xs[:, :, 0:512].rearrange("p t (h n) -> p t h n", h=8), AX, ALU.add)
            dve.drain()
            V.tensor_scalar(stat[:, 6:22], stat[:, 6:22], 1.0 / HD, EPS, ALU.mult, ALU.add)
            dve.drain()
            rsqrt(dve, stat[:, 6:22], rs[:, 6:22], rs_tmp[:, 0:16])

        def block_qk(dve, l):
            V.tensor_tensor(mqk4, mqk4, rs[:, 6:22].rearrange("p (t h) -> p t h", t=TILES).unsqueeze(3)
                            .to_broadcast([PART, TILES, 8, HD]), ALU.mult)
            dve.drain()
            for j, name in enumerate(("moba_q_g", "moba_k_g")):
                V.tensor_tensor(mqk4[:, :, 4 * j:4 * j + 4, :], mqk4[:, :, 4 * j:4 * j + 4, :],
                                B(name).unsqueeze(1).unsqueeze(1).to_broadcast([PART, TILES, 4, HD]), ALU.mult)
            dve.drain()
            rope(dve, mqk4[:, :, :, 0:8], mqk4[:, :, :, 8:16], mqk4[:, :, :, 0:8], mqk4[:, :, :, 8:16], 8, 8, 2)
            dve.sem_inc(mqk_ready, 1)

        def heads_qk(dve, l):
            dve.wait_ge(sq_ready, l + 1)
            V.tensor_reduce(stat[:, 24:32].rearrange("p (t h) -> p t h", t=TILES),
                            xs[:, :, 0:384].rearrange("p t (h n) -> p t h n", h=4), AX, ALU.add)
            V.tensor_reduce(stat[:, 32:40].rearrange("p (t h) -> p t h", t=TILES),
                            xs[:, :, 384:640].rearrange("p t (h n) -> p t h n", h=4), AX, ALU.add)
            dve.drain()
            V.tensor_scalar(stat[:, 24:32], stat[:, 24:32], 1.0 / MLA_QK, EPS, ALU.mult, ALU.add)
            V.tensor_scalar(stat[:, 32:40], stat[:, 32:40], 1.0 / MLA_NOPE, EPS, ALU.mult, ALU.add)
            dve.drain()
            rsqrt(dve, stat[:, 24:40], rs[:, 24:40], rs_tmp[:, 0:16])
            kv_ps = tp[:, 0:2, :].rearrange("p t (h n) -> p t h n", h=MLA_HEADS)
            dve.wait_ge(v_ready, l + 1)
            V.tensor_tensor(qn, tp[:, 2:4, 0:384].rearrange("p t (h n) -> p t h n", h=4),
                            rs[:, 24:32].rearrange("p (t h) -> p t h", t=TILES).unsqueeze(3)
                            .to_broadcast([PART, TILES, 4, MLA_QK]), ALU.mult)
            V.tensor_tensor(kc[:, :, :, 0:64], kv_ps[:, :, :, 0:64],
                            rs[:, 32:40].rearrange("p (t h) -> p t h", t=TILES).unsqueeze(3)
                            .to_broadcast([PART, TILES, 4, 64]), ALU.mult)
            V.tensor_copy(kc[:, :, :, 64:96], seg("kr").unsqueeze(2).to_broadcast([PART, TILES, 4, 32]))
            dve.drain()

        def heads_rope(dve, l):
            V.tensor_tensor(qn, qn, B("mla_q_g").unsqueeze(1).unsqueeze(1)
                            .to_broadcast([PART, TILES, 4, MLA_QK]), ALU.mult)
            V.tensor_tensor(kc[:, :, :, 0:64], kc[:, :, :, 0:64], B("mla_k_nope_g").unsqueeze(1).unsqueeze(1)
                            .to_broadcast([PART, TILES, 4, 64]), ALU.mult)
            dve.drain()
            rope(dve, qn[:, :, :, 64:80], qn[:, :, :, 80:96], qn[:, :, :, 64:80], qn[:, :, :, 80:96], 4, 16, 1)
            dve.sem_inc(qk_ready, 1)

        def gate_v(dve, l):
            dve.wait_ge(acc_free[0], 5 * l + 3)
            sgv, sq = seg("sg_v"), y[:, :, 256:512]
            V.tensor_reduce(stat[:, 22:24], sgv, AX, ALU.add)
            dve.drain()
            V.tensor_scalar(stat[:, 22:24], stat[:, 22:24], -1.0 / GW, None, ALU.mult)
            dve.drain()
            V.tensor_tensor(sgv, sgv, stat[:, 22:24].unsqueeze(2).to_broadcast([PART, TILES, GW]), ALU.add)
            dve.drain()
            V.tensor_tensor(sq, sgv, sgv, ALU.mult)
            dve.drain()
            V.tensor_reduce(stat[:, 22:24], sq, AX, ALU.add)
            dve.drain()
            V.tensor_scalar(stat[:, 22:24], stat[:, 22:24], 1.0 / GW, EPS, ALU.mult, ALU.add)
            dve.drain()
            rsqrt(dve, stat[:, 22:24], rs[:, 22:24], rs_tmp[:, 0:2])
            V.tensor_tensor(sgv, sgv, rs[:, 22:24].unsqueeze(2).to_broadcast([PART, TILES, GW]), ALU.mult)
            dve.drain()
            V.tensor_tensor(sgv, sgv, B("sg_ln_g").unsqueeze(1).to_broadcast([PART, TILES, GW]), ALU.mult)
            dve.drain()
            V.tensor_tensor(sgv, sgv, B("sg_ln_b").unsqueeze(1).to_broadcast([PART, TILES, GW]),
                            ALU.add).then_inc(vn_ready, 1)

        def hybrid_in(dve, l):
            scales = [MLA_QK ** -0.5] * 4 + [HD ** -0.5] * 4
            mask = C("causal")

            def at_col(h):
                return h * HD if h < 4 else 768 + (h - 4) * HD

            for i in range(len(column_chunks(D_IN))):
                if i >= 10:
                    dve_heads(dve, l, (2 * i - 20, 2 * i - 19), mask, scales, at_col)
                dve_lo(dve, HYBRID, AT_HYBRID, i + SPLIT, len(HYBRID), l)
                if i == 1:
                    latents(dve, l)
                if i == 2:
                    shared_k(dve, l)
                if i == 3:
                    latents_T(dve, l)
                if i == 4:
                    heads_qk(dve, l)
                if i == 5:
                    heads_rope(dve, l)
                if i == 6:
                    block_stats(dve, l)
                if i == 7:
                    block_qk(dve, l)
                if i == 9:
                    dve.wait_ge(sgT_ps, l + 1)
                    V.tensor_tensor(sgT, tp[:, 2, :].rearrange("p (t g n) -> p t g n", t=2, g=2),
                                    C("upto").unsqueeze(1).unsqueeze(1).to_broadcast([PART, 2, 2, 128]),
                                    ALU.mult).then_inc(sgT_ready, 1)
                    dve_masked(dve, l, 0, mask, scales)
                    dve_masked(dve, l, 1, mask, scales)
                if i == 11:
                    gate_v(dve, l)
            dve.wait_ge(acc_free[1], 4 * l + 3)
            dve.wait_ge(acc_free[0], 5 * l + 4)
            V.tensor_tensor(seg("c_h"), seg("c_h"), seg("c_c"), ALU.mult).then_inc(z_ready, 1)
            dve.drain()
            dve.wait_ge(gates_ready, l + 1)
            V.tensor_tensor(y[:, :, 0:256], y[:, :, 0:256], seg("g_a"), ALU.mult)
            V.tensor_tensor(y[:, :, 768:1024], y[:, :, 768:1024], seg("g_d"), ALU.mult)
            V.tensor_tensor(seg("c_b"), seg("c_b"), seg("g_b"), ALU.mult)
            V.tensor_tensor(seg("sg_u"), seg("sg_u"), seg("g_c"), ALU.mult)
            dve.wait_ge(conv_ps, l + 1)
            ob = y[:, :, 256:512]
            cw = B("conv_w").rearrange("p (w c) -> p w c", w=3)
            wof = [cw[:, j:j + 1, :].to_broadcast([PART, TILES, GW]) for j in range(3)]
            t_a = T[:, 0:512].rearrange("p (t n) -> p t n", t=TILES)
            V.tensor_tensor(ob, seg("c_h"), wof[2], ALU.mult)
            V.tensor_tensor(t_a, ps[:, 2, :].rearrange("p (t n) -> p t n", t=TILES), wof[1], ALU.mult)
            dve.drain()
            V.tensor_tensor(ob, ob, t_a, ALU.add)
            dve.drain()
            V.tensor_tensor(t_a, ps[:, 3, :].rearrange("p (t n) -> p t n", t=TILES), wof[0], ALU.mult)
            dve.drain()
            V.tensor_tensor(ob, ob, t_a, ALU.add)
            dve.wait_ge(mix_ps, l + 1)
            oc = y[:, :, 512:768]
            a_b = GAIN_AT["sg_b"][0]
            for t in range(TILES):
                V.tensor_tensor(oc[:, t, :].rearrange("p (g n) -> p g n", g=4),
                                ps[:, 0, t * 256:(t + 1) * 256].rearrange("p (g n) -> p g n", g=4),
                                gain[:, bass.ds(a_b + l * 4, 4)].unsqueeze(2).to_broadcast([PART, 4, 64]), ALU.add)
            dve.drain()
            V.tensor_tensor(ob, ob, seg("c_b"), ALU.mult)
            V.tensor_tensor(oc, oc, seg("sg_u"), ALU.mult).then_inc(xs_ready, 1)

        def norm_x(dve):
            norm_rows(dve, x, D, xs).then_inc(xs_ready, 1)

        def vector_program(dve):
            dve.sem_inc(layer_done, 1)
            dve.sem_inc(scat_used, 1)
            dve.wait_ge(pos_landed, 16)
            dve.wait_ge(const_landed, 16)
            two_pi = 2 * np.pi
            parts = []
            rest = two_pi
            for _ in range(3):
                m = float(2.0 ** (np.floor(np.log2(rest)) - 7))
                parts.append(float(np.floor(rest / m) * m))
                rest -= parts[-1]
            parts.append(float(np.float32(rest)))
            ang = T[:, 0:64].rearrange("p (a t n) -> p a t n", a=2, t=TILES)
            turns = T[:, 64:96].rearrange("p (t n) -> p t n", t=TILES)
            posf = T[:, 96:98]
            V.tensor_copy(posf, pos[:, :])
            dve.drain()
            V.tensor_tensor(ang[:, 1], posf.unsqueeze(2).to_broadcast([PART, TILES, 16]),
                            C("inv").unsqueeze(1).to_broadcast([PART, TILES, 16]), ALU.mult)
            dve.drain()
            round_at = 1.5 * 2.0 ** 23
            V.tensor_scalar(turns, ang[:, 1], float(1.0 / two_pi), None, ALU.mult)
            dve.drain()
            V.tensor_scalar(turns, turns, round_at, None, ALU.add)
            dve.drain()
            V.tensor_scalar(turns, turns, -round_at, None, ALU.add)
            dve.drain()
            for part in parts:
                V.scalar_tensor_tensor(out=ang[:, 1], in0=turns, scalar=-part, in1=ang[:, 1], op0=ALU.mult, op1=ALU.add)
                dve.drain()
            V.tensor_scalar(ang[:, 0], ang[:, 1], float(np.pi / 2), None, ALU.add)
            dve.drain()
            V.tensor_scalar(turns, ang[:, 0], float(np.pi), -two_pi, ALU.is_gt, ALU.mult)
            dve.drain()
            V.tensor_tensor(ang[:, 0], ang[:, 0], turns, ALU.add)
            dve.drain()
            below = float(np.nextafter(np.float32(np.pi), np.float32(0)))
            V.tensor_scalar(T[:, 0:64], T[:, 0:64], below, -below, ALU.min, ALU.max).then_inc(angle_ready, 1)
            dve_lo(dve, HYBRID, AT_HYBRID, 0)
            dve.wait_ge(x_landed, 16)
            norm_x(dve)
            dve.wait_ge(gain_ps, 1)
            V.tensor_copy(gain[:, :], tp[:, 0, 0:N_GAIN]).then_inc(gain_ready, 1)
            for i in range(1, SPLIT):
                dve_lo(dve, HYBRID, AT_HYBRID, i)
            n_in = len(column_chunks(D_IN))
            dve.wait_ge(trig_ready, 1)
            with dve.Fori(0, DEPTH) as l:
                a_g, n_g = GAIN_AT["norm_g"]
                dve_T(dve, 2 * l, l, lambda h: gain[:, bass.ds(a_g + 4 * h + l * n_g, 4)])
                hybrid_in(dve, l)
                dve_T(dve, 2 * l + 1, None, None)
                add_out(dve, HYBRID, n_in, AT_HYBRID, len(HYBRID), l)
                dve.sem_inc(layer_done, 1)
                norm_x(dve)

            def mixer(m, at):
                nT = 2 * DEPTH + 3 * m
                dve_T(dve, nT, None, lambda h: G("norm_mix_2", m)[:, 4 * h:4 * h + 4])
                n_in = len(column_chunks(D_IN2))
                att, mask, scales = DEPTH + m, C("dilated"), [HD ** -0.5] * HEADS

                def at_col(h):
                    return 512 + h * HD

                for i in range(n_in):
                    if i >= 6:
                        dve_heads(dve, att, (2 * i - 12, 2 * i - 11), mask, scales, at_col)
                    dve_lo(dve, MIXER, at, i + SPLIT)
                    if i == 5:
                        dve_masked(dve, att, 0, mask, scales)
                        dve_masked(dve, att, 1, mask, scales)
                dve_heads(dve, att, (4, 5), mask, scales, at_col)
                dve.wait_ge(z_ps, m + 1)
                for t in range(TILES):
                    V.tensor_copy(y[:, t, 0:512], ps[:, 2 + t, :])
                dve.drain()
                norm_rows(dve, y[:, :, 0:512], 512, T[:, :].rearrange("p (t n) -> p t n", t=TILES))
                dve.drain()
                V.tensor_copy(y[:, :, 0:512], T[:, :].rearrange("p (t n) -> p t n", t=TILES))
                dve_heads(dve, att, (6, 7), mask, scales, at_col)
                dve.drain()
                norm_rows(dve, y[:, :, 512:1024], 512, T[:, :].rearrange("p (t n) -> p t n", t=TILES))
                dve.drain()
                V.tensor_copy(y[:, :, 512:1024], T[:, :].rearrange("p (t n) -> p t n", t=TILES)).then_inc(xs_ready, 1)
                dve_T(dve, nT + 1, None, lambda h: G("attn_gain_2" if h else "pool_scale_2", m))
                add_out(dve, MIXER, n_in, at, last_part=m == 1)
                dve.sem_inc(layer_done, 1)

            def swiglu(chunks, n_up, at, tiles, sgb, actb, hib, lob, ups, free0, jobsn, per=0, l=0, ahead=False, between=None):
                for i in range(len(chunks)):
                    if i + SPLIT < len(chunks) or ahead:
                        dve_lo(dve, chunks, at, i + SPLIT, per, l)
                    if i < n_up and i % 4 == 3:
                        j = i // 4
                        n = chunks[i][2]
                        dve.wait_ge(split_used, number(at, i + 1, per, l))
                        dve.wait_ge(acc_free[0], free0 + j + 1)
                        if not (isinstance(jobsn, int) and jobsn + j == 0):
                            dve.wait_ge(aT_ps, jobsn + j)
                        V.tensor_tensor(actb[:, 0:tiles, 0:n], acc[:, 1, 0:tiles, 0:n], sgb[:, 0:tiles, 0:n],
                                        ALU.mult).then_inc(act_ready, 1)
                    if i >= 6 and (i - 6) % 4 == 0 and (i - 6) // 4 < ups:
                        j = (i - 6) // 4
                        nb = chunks[4 * j][2] // PART
                        w = tiles * PART
                        dve.wait_ge(ahi_ready, jobsn + j + 1)
                        src = tp[:, 2 * (j % 2):2 * (j % 2) + tiles, :].rearrange("p b n -> p (b n)")[:, 0:nb * w]
                        V.tensor_tensor(lob[:, 4 * j * w:4 * j * w + nb * w], src, hib[:, 4 * j * w:4 * j * w + nb * w],
                                        ALU.subtract).then_inc(aT_ready, 1)
                    if between:
                        between(i)

            mixer(0, AT_MIX0)
            norm_x(dve)
            dve_T(dve, 2 * DEPTH + 2, None, lambda h: G("norm_ffn_2", 0)[:, 4 * h:4 * h + 4])
            swiglu(FFN, len(FFN_UP), AT_FFN, TILES, sg, actv, ahi, alo, 6, 13, 0, ahead=True)
            dve.wait_ge(split_used, AT_FFN + len(FFN))
            for n in range(2):
                V.tensor_tensor(x[:, :, n * NC:(n + 1) * NC], x[:, :, n * NC:(n + 1) * NC], acc[:, n, :, :],
                                ALU.add).then_inc(acc_free[n], 1)
            dve.drain()
            dve.sem_inc(layer_done, 1)
            norm_x(dve)
            mixer(1, AT_MIX1)
            norm_x(dve)
            for i in range(SPLIT):
                dve_lo(dve, MOE, AT_MOE, i)
            g_ffn = G("norm_ffn_2", 1)
            for h in range(2):
                dve.wait_ge(xt_ps, 2 * (2 * DEPTH + 5) + h + 1)
                V.tensor_tensor(xT[:, 4 * h:4 * h + 4, :],
                                tp[:, 2 * h:2 * h + 2, :].rearrange("p b (c n) -> p (b c) n", c=2),
                                g_ffn[:, 4 * h:4 * h + 4].unsqueeze(2).to_broadcast([PART, 4, S]), ALU.mult).then_inc(xt_f, 1)
            dve.wait_ge(lg_ps, 1)
            V.tensor_copy(lg[:, :, :], ps[:, 0, 0:16].rearrange("p (t e) -> p t e", t=TILES))
            dve.drain()
            b4 = [PART, TILES, 8, 8]
            mine = lg[:, :, :].unsqueeze(3).to_broadcast(b4)
            other = lg[:, :, :].unsqueeze(2).to_broadcast(b4)
            bg = big[:, :, :].rearrange("p t (a b) -> p t a b", a=8)
            bg2 = big2[:, :, :].rearrange("p t (a b) -> p t a b", a=8)
            V.tensor_tensor(bg, other, mine, ALU.is_gt)
            V.tensor_tensor(bg2, other, mine, ALU.is_equal)
            V.tensor_reduce(small[:, 0:2], lg[:, :, :], AX, ALU.max)
            dve.drain()
            V.tensor_tensor(big2[:, :, :], big2[:, :, :], C("earlier").unsqueeze(1).to_broadcast([PART, TILES, 64]), ALU.mult)
            dve.drain()
            V.tensor_tensor(big[:, :, :], big[:, :, :], big2[:, :, :], ALU.add)
            dve.drain()
            V.tensor_reduce(rank[:, :, :], bg, AX, ALU.add)
            dve.drain()
            V.tensor_scalar(sel[:, :, :], rank[:, :, :], 2.0, None, ALU.is_lt).then_inc(sel_ready, 1)
            V.tensor_tensor(lg[:, :, :], lg[:, :, :], small[:, 0:2].unsqueeze(2).to_broadcast([PART, TILES, 8]),
                            ALU.subtract).then_inc(lg_ready, 1)
            dve.wait_ge(expl_ready, 1)
            V.tensor_tensor(lg[:, :, :], lg[:, :, :], sel[:, :, :], ALU.mult)
            dve.drain()
            V.tensor_reduce(small[:, 2:4], lg[:, :, :], AX, ALU.add)
            dve.drain()
            V.reciprocal(small[:, 4:6], small[:, 2:4])
            dve.drain()
            for half in range(2):
                V.tensor_tensor(gate[:, :, 8 * half:8 * half + 8], lg[:, :, :],
                                small[:, 4:6].unsqueeze(2).to_broadcast([PART, TILES, 8]), ALU.mult)
            dve.wait_ge(cnt_ps, 1)
            V.tensor_scalar(rank[:, :, :], ps[:, 1, 0:16].rearrange("p (t e) -> p t e", t=TILES), 1.0, None, ALU.add)
            V.tensor_scalar(over[:, :], ps[:, 1, 16:24], float(PART), None, ALU.is_gt)
            dve.drain()
            V.tensor_tensor(rank[:, :, :], rank[:, :, :], sel[:, :, :], ALU.mult)
            dve.drain()
            V.tensor_scalar(slot[:, :, 0:8], rank[:, :, :], -1.0, None, ALU.add)
            V.tensor_scalar(slot[:, :, 8:16], rank[:, :, :], -1.0 - PART, None, ALU.add)
            V.memset(overc[:, :], 0.0)
            V.memset(jobs_f[:, :], 0.0)
            dve.drain()
            for e in range(EXPERTS):
                V.tensor_tensor(overc[:, e + 1:e + 2], overc[:, e:e + 1], over[:, e:e + 1], ALU.add)
                dve.drain()
            for e in range(EXPERTS):
                V.tensor_scalar(big[:, 0, 0:8], C("iota")[:, 0:8], overc[:, e:e + 1], over[:, e:e + 1],
                                ALU.is_equal, ALU.mult)
                dve.drain()
                V.scalar_tensor_tensor(out=jobs_f[:, 8:16], in0=big[:, 0, 0:8], scalar=float(e), in1=jobs_f[:, 8:16],
                                       op0=ALU.mult, op1=ALU.add)
                dve.drain()
            V.tensor_copy(jobs_f[:, 0:8], C("iota")[:, 0:8])
            V.tensor_scalar(jobs_f[:, 16:17], overc[:, 8:9], float(EXPERTS), None, ALU.add)
            dve.drain()
            V.tensor_copy(jobs[:, :], jobs_f[0:1, :]).then_inc(jobs_ready, 1)
            dve.wait_ge(jobs_ready, 1)
            n_jobs = dve.value_load(jobs[0:1, 2 * EXPERTS:2 * EXPERTS + 1], min_val=EXPERTS, max_val=2 * EXPERTS)

            def pick_rows(job, col):
                for t in range(TILES):
                    V.tensor_scalar(pick[:, t, :], C("iota"), slot[:, t, bass.ds(col, 1)], None, ALU.is_equal)
                dve.drain()
                for t in range(TILES):
                    last = V.tensor_scalar(pickg[:, t, :], pick[:, t, :], gate[:, t, bass.ds(col, 1)], None, ALU.mult)
                last.then_inc(pick_ready, 1)

            def gathered(job):
                dve.wait_ge(xg_ps, job + 1)
                V.tensor_tensor(xT[:, :, 0:PART], tp[:, 0:2, :].rearrange("p b (c n) -> p (b c) n", c=4),
                                g_ffn.unsqueeze(2).to_broadcast([PART, KT, PART]), ALU.mult).then_inc(xg_f, 1)
                dve.wait_ge(xg_hi, job + 1)
                V.tensor_tensor(xlo[:, :, 0:PART], xT[:, :, 0:PART], xhi[:, :, 0:PART], ALU.subtract).then_inc(xg_lo, 1)

            pick_rows(0, 0)
            gathered(0)
            with dve.Fori(0, n_jobs) as j:
                e = dve.value_load(jobs[0:1, bass.ds(j + 1, 1)], min_val=0, max_val=2 * EXPERTS)
                col = dve.snap((e + 8 * (j + 1 >= EXPERTS)) % (2 * EXPERTS), min_val=0, max_val=2 * EXPERTS - 1)

                def between(i):
                    if i == BACK_AT + 1:
                        dve.wait_ge(back_ps, j + 1)
                        pick_rows(j + 1, col)
                    if i == GATHER_AT:
                        gathered(j + 1)

                swiglu(MOE, len(MOE_UP), AT_MOE, 1, sg2, actv2, ahi2, alo2, 7, 23 + 8 * j, 6 + 7 * j, len(MOE), j,
                       ahead=True, between=between)
                dve.wait_ge(scat_ps, j + 1)
                V.tensor_tensor(x[:, :, :], x[:, :, :], tp.rearrange("p (t n) c -> p t (n c)", t=TILES),
                                ALU.add).then_inc(scat_used, 1)
                dve.drain()
            norm_rows(dve, x, D, xs)
            dve.drain()
            dve.wait_ge(small_landed, small_at(DEPTH, 4))
            V.tensor_tensor(y[:, :, :], xs[:, :, :], fin_g[:, :].unsqueeze(1).to_broadcast([PART, TILES, D]),
                            ALU.mult).then_inc(y_ready, 1)

        mm = nc.tensor.matmul

        def pe_chunk(pe, chunk, c0, i, banks, lhs, tiles, first, last, per=0, l=0):
            _, _, n, k0, k = chunk
            pe.wait_ge(lo_ready, number(c0, i + 1, per, l))
            for t in range(tiles):
                for c in range(k):
                    hi, lo = lhs(k0 + c, t)
                    out = banks[:, t, 0:n]
                    mm(out, lo, whi[i % SPLIT][:, c, 0:n], start=first and c == 0, stop=False)
                    mm(out, hi, wlo[i % SPLIT][:, c, 0:n], start=False, stop=False)
                    op = mm(out, hi, whi[i % SPLIT][:, c, 0:n], start=False, stop=last and c == k - 1)
            op.then_inc(split_used, 1)
            return op

        def x_lhs(k, t):
            return xhi[:, k, t * PART:(t + 1) * PART], xlo[:, k, t * PART:(t + 1) * PART]

        def pe_linear(pe, chunks, i0, i1, c0, free, per=0, l=0, between=None):
            for i in range(i0, i1):
                g = i // 2
                if i % 2 == 0:
                    v = free(g)
                    if v is not None:
                        pe.wait_ge(acc_free[g % 2], v)
                pe_chunk(pe, chunks[i], c0, i, acc[:, g % 2], x_lhs, TILES, i % 2 == 0, i % 2 == 1, per, l)
                if between:
                    between(i)

        def pe_T(pe, nT):
            pe.wait_ge(xs_ready, nT + 1)
            for c in range(KT):
                for t in range(TILES):
                    op = nc.tensor.transpose(tp[:, c // 2, (c % 2) * S + t * PART:(c % 2) * S + (t + 1) * PART],
                                             xs[:, t, c * PART:(c + 1) * PART], ident)
                if c in (3, 7):
                    op.then_inc(xt_ps, 1)

        def pe_scores(pe, att, h, qk):
            if h >= 2:
                pe.wait_ge(s_masked, HEADS * att + h - 1)
            q, k = qk(h)
            mm(tp[:, h % 2, 0:128], q[:, 0:128], k[:, 0:128], start=True, stop=True)
            mm(tp[:, h % 2, 128:384], q[:, 128:256], k[:, :], start=True, stop=True).then_inc(s_ps, 1)

        def pe_heads(pe, att, heads, qk, v):
            for h in heads:
                pe.wait_ge(p_ready, HEADS * att + h + 1)
                if h >= 1:
                    pe.wait_ge(pT_ready, HEADS * att + h)
                for b in range(3):
                    op = nc.tensor.transpose(tp[:, 2, 128 * b:128 * b + 128], pr[:, h % 2, 128 * b:128 * b + 128],
                                             ident)
                op.then_inc(pT_ps, 1)
                if h + 2 < HEADS:
                    pe_scores(pe, att, h + 2, qk)
                pe.wait_ge(pT_ready, HEADS * att + h + 1)
                if h >= 1:
                    pe.wait_ge(o_ready, HEADS * att + h)
                mm(tp[:, 3, 0:HD], pT[:, 0:128], v(h, 0), start=True, stop=True)
                mm(tp[:, 3, HD:2 * HD], pT[:, 128:256], v(h, 0), start=True, stop=False)
                mm(tp[:, 3, HD:2 * HD], pT[:, 256:384], v(h, 1), start=False, stop=True).then_inc(o_ps, 1)

        def tensor_program(pe):
            pe.wait_ge(const_landed, 16)
            pe.wait_ge(rows_landed, 16 * len(GAIN_ROWS))
            nc.tensor.transpose(tp[:, 0, 0:N_GAIN], g_rows, ident[0:N_GAIN, 0:N_GAIN]).then_inc(gain_ps, 1)
            pe.wait_ge(gain_ready, 1)
            n_in = len(column_chunks(D_IN))
            with pe.Fori(0, DEPTH) as l:
                pe_T(pe, 2 * l)
                pe.wait_ge(xt_lo, 4 * l + 2)

                def free(g):
                    if g < 2:
                        return None
                    return g // 2 + (5 if g % 2 == 0 else 4) * l

                def qk(h):
                    if h < 4:
                        return QT[0:96, h, :], KTr[0:96, h, :]
                    b = (h % 2) * HD
                    return QT[b:b + HD, 2 + h // 2, :], KTr[b:b + HD, 2 + h // 2, :]

                def v(h, t):
                    return (va if h < 4 else seg("mv"))[:, t, (h % 4) * HD:(h % 4 + 1) * HD]

                def between(i):
                    if i == 3:
                        pe.wait_ge(cn_ready, l + 1)
                        for c in range(3):
                            for t in range(TILES):
                                op = nc.tensor.transpose(
                                    tp[:, c // 2, (c % 2) * S + t * PART:(c % 2) * S + (t + 1) * PART],
                                    P[:, t, c * PART:(c + 1) * PART], ident)
                        op.then_inc(cT_ps, 1)
                    if i == 4:
                        pe.wait_ge(small_landed, 16 * N_SMALL * (l + 1))
                        pe.wait_ge(cT_ready, l + 1)
                        for t in range(TILES):
                            for c in range(2):
                                mm(tp[:, 2 + t, 0:384], cT[:, c, t * PART:(t + 1) * PART], w_uq[:, c, :],
                                   start=c == 0, stop=c == 1)
                            op = mm(tp[:, t, :], cT[:, 2, t * PART:(t + 1) * PART], w_ukv[:, :], start=True, stop=True)
                        op.then_inc(qkv_ps, 1)
                    if i == 6:
                        pe.wait_ge(qk_ready, l + 1)
                        for src, bank in ((qn, 4), (kc, 6)):
                            for h in range(4):
                                for t in range(TILES):
                                    op = nc.tensor.transpose(
                                        ps[0:96, bank + h // 2, (h % 2) * S + t * PART:(h % 2) * S + (t + 1) * PART],
                                        src[:, t, h, :], ident)
                            op.then_inc(qT_ps, 1)
                    if i == 8:
                        pe.wait_ge(mqk_ready, l + 1)
                        pe.wait_ge(qT_ready, 4 * l + 2)
                        for name, bank in (("mq", 4), ("mk", 5)):
                            for c in range(2):
                                for t in range(TILES):
                                    a = COLS[name][0] + c * PART
                                    op = nc.tensor.transpose(ps[:, bank, c * S + t * PART:c * S + (t + 1) * PART],
                                                             P[:, t, a:a + PART], ident)
                            op.then_inc(qT_ps, 1)
                        for g in range(4):
                            op = nc.tensor.transpose(tp[:, 2, g * 128:(g + 1) * 128], sgw[:, g, :], ident)
                        op.then_inc(sgT_ps, 1)
                    if i == 9:
                        pe.wait_ge(qT_ready, 4 * l + 4)
                        pe_scores(pe, l, 0, qk)
                        pe_scores(pe, l, 1, qk)
                        pe.wait_ge(sgT_ready, l + 1)
                    if i >= 10:
                        pe_heads(pe, l, (2 * i - 20, 2 * i - 19), qk, v)

                pe_linear(pe, HYBRID, 0, n_in, AT_HYBRID, free, len(HYBRID), l, between)
                pe.wait_ge(vn_ready, l + 1)
                pe.wait_ge(acc_free[0], 5 * l + 4)
                for t in range(TILES):
                    for g in range(4):
                        a = COLS["sg_v"][0] + g * 64
                        op = mm(ps[:, 0, t * 256 + g * 64:t * 256 + g * 64 + 64], sgT[:, g // 2, g % 2, :],
                                P[:, t, a:a + 64], start=True, stop=True)
                op.then_inc(mix_ps, 1)
                pe.wait_ge(z_ready, l + 1)
                z = seg("c_h")
                for j in range(2):
                    mm(ps[:, 2 + j, 0:GW], shift[:, 2 * j, :], z[:, 0, :], start=True, stop=True)
                    mm(ps[:, 2 + j, GW:2 * GW], shift[:, 2 * j, :], z[:, 1, :], start=True, stop=False)
                    op = mm(ps[:, 2 + j, GW:2 * GW], shift[:, 2 * j + 1, :], z[:, 0, :], start=False, stop=True)
                op.then_inc(conv_ps, 1)
                pe_T(pe, 2 * l + 1)
                pe.wait_ge(xt_lo, 4 * l + 4)
                pe_linear(pe, HYBRID, n_in, len(HYBRID), AT_HYBRID, free, len(HYBRID), l)

            def mixer(m, at, free0, free1):
                nT = 2 * DEPTH + 3 * m
                pe_T(pe, nT)
                pe.wait_ge(xt_lo, 2 * nT + 2)

                def free(g):
                    return (free1 if g % 2 else free0) + g // 2
                n_in = len(column_chunks(D_IN2))

                def qk(h):
                    b = (h % 2) * HD
                    return QT[b:b + HD, h // 2, :], KTr[b:b + HD, h // 2, :]

                def v(h, t):
                    return P[:, t, 1536 + h * HD:1536 + (h + 1) * HD]

                def between(i):
                    if i == 4:
                        pe.wait_ge(acc_free[0], free0 + 1)
                        pe.wait_ge(acc_free[1], free1 + 1)
                        for src, bank in ((512, 4), (1024, 6)):
                            for c in range(4):
                                for t in range(TILES):
                                    op = nc.tensor.transpose(
                                        ps[:, bank + c // 2, (c % 2) * S + t * PART:(c % 2) * S + (t + 1) * PART],
                                        P[:, t, src + c * PART:src + (c + 1) * PART], ident)
                            op.then_inc(qT_ps, 1)
                    if i == 5:
                        pe.wait_ge(qT_ready, 4 * DEPTH + 2 * m + 2)
                        pe_scores(pe, DEPTH + m, 0, qk)
                        pe_scores(pe, DEPTH + m, 1, qk)
                        pe.wait_ge(acc_free[0], free0 + 2)
                    if i >= 6:
                        pe_heads(pe, DEPTH + m, (2 * i - 12, 2 * i - 11), qk, v)

                pe_linear(pe, MIXER, 0, n_in, at, free, between=between)
                pe.wait_ge(acc_free[1], free1 + 2)
                for g in range(4):
                    o = (g % 2) * S
                    mm(ps[:, g // 2, o:o + PART], P[:, 0, g * PART:(g + 1) * PART], poolm[:, g, 0, :],
                       start=True, stop=True)
                    mm(ps[:, g // 2, o + PART:o + S], P[:, 0, g * PART:(g + 1) * PART], poolm[:, g, 1, :],
                       start=True, stop=False)
                    op = mm(ps[:, g // 2, o + PART:o + S], P[:, 1, g * PART:(g + 1) * PART], poolm[:, g, 2, :],
                            start=False, stop=True)
                op.then_inc(dT_ps, 1)
                pe_heads(pe, DEPTH + m, (4, 5), qk, v)
                pe.wait_ge(dT_ready, m + 1)
                pe.wait_ge(small_landed, small_at(DEPTH, m + 1))
                dT = T[:, :].rearrange("p (g t) -> p g t", g=4)
                for t in range(TILES):
                    for g in range(4):
                        op = mm(ps[:, 2 + t, g * PART:(g + 1) * PART], dT[:, g, t * PART:(t + 1) * PART], sgw[:, g, :],
                                start=True, stop=True)
                op.then_inc(z_ps, 1)
                pe_heads(pe, DEPTH + m, (6, 7), qk, v)
                pe_T(pe, nT + 1)
                pe.wait_ge(xt_lo, 2 * nT + 4)
                pe_linear(pe, MIXER, n_in, len(MIXER), at, free)

            def swiglu(chunks, n_up, at, tiles, actb, hib, lob, ups, free0, free1, jobsn, per=0, l=0, between=None,
                   before_T=None):
                w = tiles * PART

                def a_lhs(k, t):
                    a = k * w + t * PART
                    return hib[:, a:a + PART], lob[:, a:a + PART]

                last_k = (len(chunks) - n_up) // 2 - 1
                for i in range(len(chunks)):
                    if i < n_up:
                        g = i // 2 % 2
                        if i % 4 == 0:
                            pe.wait_ge(acc_free[0], free0 + i // 4)
                        elif i == 2:
                            pe.wait_ge(acc_free[1], free1)
                        elif i % 4 == 2:
                            pe.wait_ge(act_ready, jobsn + i // 4)
                        pe_chunk(pe, chunks[i], at, i, acc[:, g], x_lhs, tiles, i % 2 == 0, i % 2 == 1, per, l)
                    else:
                        kq, n = (i - n_up) // 2, (i - n_up) % 2
                        if kq == 0 and n == 0:
                            pe.wait_ge(acc_free[0], free0 + n_up // 4)
                        elif kq == 0:
                            pe.wait_ge(act_ready, jobsn + n_up // 4)
                        if n == 0:
                            pe.wait_ge(aT_ready, jobsn + kq + 1)
                        pe_chunk(pe, chunks[i], at, i, acc[:, n], a_lhs, tiles, kq == 0, kq == last_k, per, l)
                    if i >= 6 and (i - 6) % 4 == 0 and (i - 6) // 4 < ups:
                        j = (i - 6) // 4
                        pe.wait_ge(act_ready, jobsn + j + 1)
                        if j >= 2:
                            pe.wait_ge(aT_ready, jobsn + j - 1)
                        elif before_T:
                            before_T()
                        flat = tp[:, 2 * (j % 2):2 * (j % 2) + tiles, :].rearrange("p b n -> p (b n)")
                        for b in range(chunks[4 * j][2] // PART):
                            for t in range(tiles):
                                a = b * w + t * PART
                                op = nc.tensor.transpose(flat[:, a:a + PART], actb[:, t, b * PART:(b + 1) * PART], ident)
                        op.then_inc(aT_ps, 1)
                    if between:
                        between(i)

            mixer(0, AT_MIX0, 10, 8)
            pe_T(pe, 2 * DEPTH + 2)
            pe.wait_ge(xt_lo, 2 * (2 * DEPTH + 2) + 2)
            swiglu(FFN, len(FFN_UP), AT_FFN, TILES, actv, ahi, alo, 6, 13, 11, 0)
            mixer(1, AT_MIX1, 20, 12)
            pe_T(pe, 2 * DEPTH + 5)
            pe.wait_ge(small_landed, small_at(DEPTH, 4))
            pe.wait_ge(xt_f, 2 * (DEPTH + 2 * DEPTH + 5 - 2 * DEPTH) + 2)
            for t in range(TILES):
                for c in range(KT):
                    op = mm(ps[:, 0, t * 8:(t + 1) * 8], xT[:, c, t * PART:(t + 1) * PART], w_rt[:, c, :],
                            start=c == 0, stop=c == KT - 1)
            op.then_inc(lg_ps, 1)
            pe.wait_ge(sel_ready, 1)
            mm(ps[:, 1, 0:8], C("before"), sel[:, 0, :], start=True, stop=True)
            mm(ps[:, 1, 8:16], C("ones"), sel[:, 0, :], start=True, stop=False)
            mm(ps[:, 1, 8:16], C("before"), sel[:, 1, :], start=False, stop=True)
            mm(ps[:, 1, 16:24], C("ones"), sel[:, 0, :], start=True, stop=False)
            mm(ps[:, 1, 16:24], C("ones"), sel[:, 1, :], start=False, stop=True).then_inc(cnt_ps, 1)
            pe.wait_ge(jobs_ready, 1)
            n_jobs = pe.value_load(jobs[0:1, 2 * EXPERTS:2 * EXPERTS + 1], min_val=EXPERTS, max_val=2 * EXPERTS)

            def gather(job):
                pe.wait_ge(pick_ready, job + 1)
                for c in range(KT):
                    for t in range(TILES):
                        op = mm(tp[:, c // 4, (c % 4) * PART:(c % 4 + 1) * PART], xs[:, t, c * PART:(c + 1) * PART],
                                pick[:, t, :], start=t == 0, stop=t == TILES - 1)
                op.then_inc(xg_ps, 1)

            gather(0)
            with pe.Fori(0, n_jobs) as j:
                pe.wait_ge(xg_lo, j + 1)

                def between(i):
                    if i == BACK_AT:
                        pe.wait_ge(aT_ready, 6 + 7 * j + 7)
                        for t in range(TILES):
                            op = nc.tensor.transpose(tp[:, 2, t * PART:(t + 1) * PART], pickg[:, t, :], ident)
                        op.then_inc(back_ps, 1)
                    if i == GATHER_AT - 2:
                        gather(j + 1)

                swiglu(MOE, len(MOE_UP), AT_MOE, 1, actv2, ahi2, alo2, 7, 23 + 8 * j, 15 + j, 6 + 7 * j,
                       len(MOE), j, between=between, before_T=lambda: pe.wait_ge(scat_used, j + 1))
                pe.wait_ge(back_ready, j + 1)
                pe.wait_ge(acc_free[1], 15 + j + 1)
                for t in range(TILES):
                    for n in range(2):
                        op = mm(tp[:, 2 * t + n, :], backT[:, t, :], yg[:, n * NC:(n + 1) * NC], start=True, stop=True)
                op.then_inc(scat_ps, 1)

        with nc.Block() as block:
            @block.sync
            def _(sp):
                sync_program(sp)

            @block.gpsimd
            def _(pool):
                pool_program(pool)

            @block.scalar
            def _(act):
                scalar_program(act)

            @block.vector
            def _(dve):
                vector_program(dve)

            @block.tensor
            def _(pe):
                tensor_program(pe)


_INS = ["x", "positions", "norm_g", "w_in", "mla_q_norm_g", "mla_w_uq", "mla_kv_norm_g", "mla_w_ukv", "mla_q_g",
        "mla_k_nope_g", "mla_k_rope_g", "conv_w", "sg_ln_g", "sg_ln_b", "sg_w", "sg_b", "moba_q_g", "moba_k_g",
        "w_out", "norm_mix_2", "w_in_2", "w_pool_2", "pool_scale_2", "attn_gain_2", "w_out_2", "norm_ffn_2",
        "ffn_wg_2", "ffn_wu_2", "ffn_wd_2", "w_router_2", "moe_wg_2", "moe_wu_2", "moe_wd_2", "final_norm_2"]


def kernel(**inputs):
    import concourse.bacc as bacc
    from concourse.bass_utils import run_bass_kernel_spmd

    nc = bacc.Bacc("TRN2", target_bir_lowering=False, num_devices=1)
    arrays, aps = {}, {}
    for name in _INS:
        a = np.ascontiguousarray(inputs[name])
        arrays[name] = a
        aps[name] = nc.dram_tensor(name, a.shape, mybir.dt.from_np(a.dtype), kind="ExternalInput").ap()
    arrays["consts"] = shape_constants()
    aps["consts"] = nc.dram_tensor("consts", arrays["consts"].shape, F32, kind="ExternalInput").ap()
    aps["out"] = nc.dram_tensor("out", (1, S, D), F32, kind="ExternalOutput").ap()
    build(nc, aps)
    r = run_bass_kernel_spmd(nc, [arrays], core_ids=[0])
    return r.results[0]["out"]
```
